# Optimizing a Trainium2 kernel written in Bass

```python
import math
import jax, jax.numpy as jnp
from jax import lax
import numpy as np
import jax
import jax.numpy as jnp

D_MODEL = 1024
BATCH = 1
SEQ = 256
DEPTH = 2

HEAD_DIM = 64
MEM_LEN = 256
MEM_HEADS = 4
MEM_WIDTH = MEM_HEADS * HEAD_DIM
MIX_WIDTH = D_MODEL
CONV_CH = MIX_WIDTH - MEM_WIDTH
CONV_WIDTH = 31
SWA_Q_HEADS = 12
SWA_KV_HEADS = 4
SWA_GROUP = SWA_Q_HEADS // SWA_KV_HEADS
SWA_Q_WIDTH = SWA_Q_HEADS * HEAD_DIM
SWA_KV_WIDTH = SWA_KV_HEADS * HEAD_DIM
WINDOW = 128
BLOCK = 128
D_FF_DENSE = 2816
N_EXPERTS = 8
TOP_K = 2
D_FF_EXPERT = 3584
N_EVEN = (DEPTH + 1) // 2
N_ODD = DEPTH // 2
RMS_EPS = 1e-6
LN_EPS = 1e-5
ALIBI_MAX_BIAS = 8.0
NEG_INF = -1e30


def rms_norm(x, g):
    xf = x.astype(jnp.float32)
    y = xf * lax.rsqrt(jnp.mean(xf * xf, axis=-1, keepdims=True) + RMS_EPS)
    return (y * g.astype(jnp.float32)).astype(x.dtype)

def layer_norm(x, g, b):
    xf = x.astype(jnp.float32)
    mu = jnp.mean(xf, axis=-1, keepdims=True)
    var = jnp.mean(jnp.square(xf - mu), axis=-1, keepdims=True)
    y = (xf - mu) * lax.rsqrt(var + LN_EPS)
    return (y * g.astype(jnp.float32) + b.astype(jnp.float32)).astype(x.dtype)

def swiglu(h, w_gate, w_up, w_down):
    return (jax.nn.silu(h @ w_gate) * (h @ w_up)) @ w_down

def alibi_slopes(n_heads):
    return jnp.exp2(-ALIBI_MAX_BIAS * (jnp.arange(n_heads, dtype=jnp.float32) + 1.0) / n_heads)

def memory_attention(q, q_g, mem_k, mem_v):
    b, s, _ = q.shape
    q = rms_norm(q.reshape(b, s, MEM_HEADS, HEAD_DIM), q_g)
    sc = jnp.einsum('bshd,bmhd->bhsm', q, mem_k).astype(jnp.float32) * (HEAD_DIM ** -0.5)
    p = jax.nn.softmax(sc, axis=-1).astype(mem_v.dtype)
    o = jnp.einsum('bhsm,bmhd->bshd', p, mem_v)
    return o.reshape(b, s, MEM_WIDTH)

def conv_mixer(h, w_in, b_glu, dw_w, dw_b, ln_g, ln_b, memq_g, w_out, mem_k, mem_v):
    proj = h @ w_in
    a = proj[..., :CONV_CH] + b_glu[:CONV_CH]
    gate = proj[..., CONV_CH:2 * CONV_CH] + b_glu[CONV_CH:]
    q_mem = proj[..., 2 * CONV_CH:]
    u = a * jax.nn.sigmoid(gate)
    u_pad = jnp.pad(u, ((0, 0), (CONV_WIDTH - 1, 0), (0, 0)))
    c = lax.conv_general_dilated(
        u_pad, dw_w[:, None, :], window_strides=(1,), padding='VALID',
        dimension_numbers=('NWC', 'WIO', 'NWC'), feature_group_count=CONV_CH) + dw_b
    c = jax.nn.silu(layer_norm(c, ln_g, ln_b))
    m = memory_attention(q_mem, memq_g, mem_k, mem_v)
    return jnp.concatenate([c, m], axis=-1) @ w_out

def swa_mixer(h, w_in, q_g, k_g, sinks, memq_g, w_out, mem_k, mem_v):
    b, s, _ = h.shape
    nb = s // BLOCK
    proj = h @ w_in
    o1 = SWA_Q_WIDTH
    o2 = o1 + SWA_KV_WIDTH
    o3 = o2 + SWA_KV_WIDTH
    q = rms_norm(proj[..., :o1].reshape(b, s, SWA_KV_HEADS, SWA_GROUP, HEAD_DIM), q_g)
    k = rms_norm(proj[..., o1:o2].reshape(b, s, SWA_KV_HEADS, HEAD_DIM), k_g)
    v = proj[..., o2:o3].reshape(b, s, SWA_KV_HEADS, HEAD_DIM)
    q_mem = proj[..., o3:]

    qb = q.reshape(b, nb, BLOCK, SWA_KV_HEADS, SWA_GROUP, HEAD_DIM)
    def band(t):
        prev = jnp.pad(t, ((0, 0), (BLOCK, 0), (0, 0), (0, 0)))[:, :s]
        return jnp.concatenate([prev.reshape(b, nb, BLOCK, SWA_KV_HEADS, HEAD_DIM),
                                t.reshape(b, nb, BLOCK, SWA_KV_HEADS, HEAD_DIM)], axis=2)
    kk = band(k)
    vv = band(v)
    sc = jnp.einsum('bnqhgd,bnchd->bnhgqc', qb, kk).astype(jnp.float32) * (HEAD_DIM ** -0.5)

    qpos = jnp.arange(BLOCK) + BLOCK
    kpos = jnp.arange(2 * BLOCK)
    dist = (qpos[:, None] - kpos[None, :]).astype(jnp.float32)
    win = (dist >= 0) & (dist < WINDOW)
    first = (jnp.arange(nb)[:, None] > 0) | (kpos[None, :] >= BLOCK)
    mask = win[None, :, :] & first[:, None, :]
    slopes = alibi_slopes(SWA_Q_HEADS).reshape(SWA_KV_HEADS, SWA_GROUP)
    bias = -slopes[:, :, None, None] * dist[None, None]
    sc = jnp.where(mask[None, :, None, None], sc + bias[None, None], NEG_INF)

    sink = jnp.broadcast_to(sinks.astype(jnp.float32).reshape(1, 1, SWA_KV_HEADS, SWA_GROUP, 1, 1),
                            sc.shape[:-1] + (1,))
    p = jax.nn.softmax(jnp.concatenate([sc, sink], axis=-1), axis=-1)[..., :-1]
    o = jnp.einsum('bnhgqc,bnchd->bnqhgd', p.astype(vv.dtype), vv).reshape(b, s, SWA_Q_WIDTH)
    m = memory_attention(q_mem, memq_g, mem_k, mem_v)
    return jnp.concatenate([o, m], axis=-1) @ w_out

def moe_swiglu(h, router, we_gate, we_up, we_down):
    logits = (h @ router).astype(jnp.float32)
    top_v, top_i = lax.top_k(logits, TOP_K)
    top_w = jax.nn.softmax(top_v, axis=-1)
    gates = jnp.sum(jax.nn.one_hot(top_i, N_EXPERTS, dtype=jnp.float32) * top_w[..., None], axis=-2)
    gates = gates.astype(h.dtype)
    out = jnp.zeros_like(h)
    for e in range(N_EXPERTS):
        out = out + gates[..., e:e + 1] * swiglu(h, we_gate[e], we_up[e], we_down[e])
    return out

def first_inputs(seed: int = 0) -> dict:
    key = jax.random.key(seed)
    ks = iter(jax.random.split(key, 40))
    f32 = jnp.float32
    def nrm(shape, scale):
        return jax.random.normal(next(ks), shape, f32) * scale
    def gain(shape):
        return 1.0 + 0.05 * jax.random.normal(next(ks), shape, f32)
    D = D_MODEL
    return {
        "x": nrm((BATCH, SEQ, D), 1.0),
        "mem": nrm((BATCH, MEM_LEN, D), 1.0),
        "mem_norm_g": gain((D,)),
        "w_mem_kv": nrm((D, 2 * MEM_WIDTH), D ** -0.5),
        "mem_k_norm_g": gain((HEAD_DIM,)),
        "cv_attn_norm_g": gain((N_EVEN, D)),
        "cv_w_in": nrm((N_EVEN, D, 2 * CONV_CH + MEM_WIDTH), D ** -0.5),
        "cv_b_glu": nrm((N_EVEN, 2 * CONV_CH), 0.02),
        "cv_dw_w": nrm((N_EVEN, CONV_WIDTH, CONV_CH), CONV_WIDTH ** -0.5),
        "cv_dw_b": nrm((N_EVEN, CONV_CH), 0.02),
        "cv_ln_g": gain((N_EVEN, CONV_CH)),
        "cv_ln_b": nrm((N_EVEN, CONV_CH), 0.02),
        "cv_memq_norm_g": gain((N_EVEN, HEAD_DIM)),
        "cv_w_out": nrm((N_EVEN, MIX_WIDTH, D), MIX_WIDTH ** -0.5),
        "cv_ffn_norm_g": gain((N_EVEN, D)),
        "cv_w_gate": nrm((N_EVEN, D, D_FF_DENSE), D ** -0.5),
        "cv_w_up": nrm((N_EVEN, D, D_FF_DENSE), D ** -0.5),
        "cv_w_down": nrm((N_EVEN, D_FF_DENSE, D), D_FF_DENSE ** -0.5),
        "sw_attn_norm_g": gain((N_ODD, D)),
        "sw_w_in": nrm((N_ODD, D, SWA_Q_WIDTH + 2 * SWA_KV_WIDTH + MEM_WIDTH), D ** -0.5),
        "sw_q_norm_g": gain((N_ODD, HEAD_DIM)),
        "sw_k_norm_g": gain((N_ODD, HEAD_DIM)),
        "sw_sinks": nrm((N_ODD, SWA_Q_HEADS), 0.5),
        "sw_memq_norm_g": gain((N_ODD, HEAD_DIM)),
        "sw_w_out": nrm((N_ODD, MIX_WIDTH, D), MIX_WIDTH ** -0.5),
        "sw_ffn_norm_g": gain((N_ODD, D)),
        "sw_router": nrm((N_ODD, D, N_EXPERTS), D ** -0.5),
        "sw_we_gate": nrm((N_ODD, N_EXPERTS, D, D_FF_EXPERT), D ** -0.5),
        "sw_we_up": nrm((N_ODD, N_EXPERTS, D, D_FF_EXPERT), D ** -0.5),
        "sw_we_down": nrm((N_ODD, N_EXPERTS, D_FF_EXPERT, D), D_FF_EXPERT ** -0.5),
    }

def first_block(x, mem, mem_norm_g, w_mem_kv, mem_k_norm_g,
              cv_attn_norm_g, cv_w_in, cv_b_glu, cv_dw_w, cv_dw_b, cv_ln_g, cv_ln_b,
              cv_memq_norm_g, cv_w_out, cv_ffn_norm_g, cv_w_gate, cv_w_up, cv_w_down,
              sw_attn_norm_g, sw_w_in, sw_q_norm_g, sw_k_norm_g, sw_sinks, sw_memq_norm_g,
              sw_w_out, sw_ffn_norm_g, sw_router, sw_we_gate, sw_we_up, sw_we_down):
    b, m_len, _ = mem.shape
    mkv = rms_norm(mem, mem_norm_g) @ w_mem_kv
    mem_k = rms_norm(mkv[..., :MEM_WIDTH].reshape(b, m_len, MEM_HEADS, HEAD_DIM), mem_k_norm_g)
    mem_v = mkv[..., MEM_WIDTH:].reshape(b, m_len, MEM_HEADS, HEAD_DIM)

    h = x
    for i in range(DEPTH):
        j = i // 2
        if i % 2 == 0:
            hn = rms_norm(h, cv_attn_norm_g[j])
            h = h + conv_mixer(hn, cv_w_in[j], cv_b_glu[j], cv_dw_w[j], cv_dw_b[j], cv_ln_g[j],
                               cv_ln_b[j], cv_memq_norm_g[j], cv_w_out[j], mem_k, mem_v)
            hn = rms_norm(h, cv_ffn_norm_g[j])
            h = h + swiglu(hn, cv_w_gate[j], cv_w_up[j], cv_w_down[j])
        else:
            hn = rms_norm(h, sw_attn_norm_g[j])
            h = h + swa_mixer(hn, sw_w_in[j], sw_q_norm_g[j], sw_k_norm_g[j], sw_sinks[j],
                              sw_memq_norm_g[j], sw_w_out[j], mem_k, mem_v)
            hn = rms_norm(h, sw_ffn_norm_g[j])
            h = h + moe_swiglu(hn, sw_router[j], sw_we_gate[j], sw_we_up[j], sw_we_down[j])
    return h


ROT_DIM = HEAD_DIM // 4
ROPE_THETA = 500000.0
DIL_GROUPS = ((128, 1), (512, 4), (2048, 16))
HEADS_PER_DIL_GROUP = 2
N_HEADS_A = len(DIL_GROUPS) * HEADS_PER_DIL_GROUP
N_HEADS_B = 6
N_HEADS_M = 4
MOBA_BLOCK = 256
MOBA_TOPK = 3
MOBA_Q_CHUNK = 32
N_MEM = 256
D_FF = 4 * D_MODEL
N_BRANCH = 3
WIDTH_A = N_HEADS_A * HEAD_DIM
WIDTH_A_OUT = HEADS_PER_DIL_GROUP * HEAD_DIM
WIDTH_B = N_HEADS_B * HEAD_DIM
WIDTH_M = N_HEADS_M * HEAD_DIM
D_IN = 3 * WIDTH_A + 3 * WIDTH_B + WIDTH_M + N_BRANCH * D_MODEL
NEG_INF_2 = -1e30


def rms_norm_2(x, g):
    xf = x.astype(jnp.float32)
    y = xf * lax.rsqrt(jnp.mean(xf * xf, axis=-1, keepdims=True) + RMS_EPS)
    return (y * g.astype(jnp.float32)).astype(x.dtype)

def partial_rope(x, pos):
    inv_freq = 1.0 / (ROPE_THETA ** (jnp.arange(0, ROT_DIM, 2, dtype=jnp.float32) / ROT_DIM))
    ang = pos.astype(jnp.float32)[:, None] * inv_freq[None, :]
    cos = jnp.cos(ang)[None, :, None, :]
    sin = jnp.sin(ang)[None, :, None, :]
    xr = x[..., :ROT_DIM].astype(jnp.float32)
    x1, x2 = xr[..., :ROT_DIM // 2], xr[..., ROT_DIM // 2:]
    rot = jnp.concatenate([x1 * cos - x2 * sin, x2 * cos + x1 * sin], axis=-1).astype(x.dtype)
    return jnp.concatenate([rot, x[..., ROT_DIM:]], axis=-1)

def dilated_window_attn(q, k, v, window, dilation):
    B, S, H, Dh = q.shape
    n = window // dilation
    span = n * dilation
    Sp = -(-S // span) * span
    L = Sp // dilation
    nblk = L // n

    def to_blocks(t):
        t = jnp.pad(t, ((0, 0), (0, Sp - S), (0, 0), (0, 0)))
        t = t.reshape(B, L, dilation, H, Dh).transpose(0, 2, 3, 1, 4)
        return t.reshape(B, dilation, H, nblk, n, Dh)

    def with_prev(t):
        prev = jnp.pad(t, ((0, 0), (0, 0), (0, 0), (1, 0), (0, 0), (0, 0)))[:, :, :, :-1]
        return jnp.concatenate([prev, t], axis=-2)

    qb = to_blocks(q)
    kk = with_prev(to_blocks(k))
    vv = with_prev(to_blocks(v))
    s = jnp.einsum('brhnqd,brhnkd->brhnqk', qb, kk).astype(jnp.float32)
    i = jnp.arange(n)[:, None]
    j = jnp.arange(2 * n)[None, :]
    band = (j >= i) & (j <= i + n)
    first = (jnp.arange(nblk) == 0)[:, None, None] & (j < n)[None]
    mask = band[None] & ~first
    s = jnp.where(mask, s, NEG_INF_2)
    mx = jnp.max(s, axis=-1, keepdims=True)
    p = jnp.exp(s - mx)
    den = jnp.sum(p, axis=-1, keepdims=True)
    o = jnp.einsum('brhnqk,brhnkd->brhnqd', (p / den).astype(v.dtype), vv)
    lse = (mx + jnp.log(den))[..., 0]
    o = o.reshape(B, dilation, H, L, Dh).transpose(0, 3, 1, 2, 4).reshape(B, Sp, H, Dh)[:, :S]
    lse = lse.reshape(B, dilation, H, L).transpose(0, 3, 1, 2).reshape(B, Sp, H)[:, :S]
    return o, lse

def dilated_mixer(q, k, v):
    B, S = q.shape[0], q.shape[1]
    outs, lses = [], []
    for g, (win, dil) in enumerate(DIL_GROUPS):
        sl = slice(g * HEADS_PER_DIL_GROUP, (g + 1) * HEADS_PER_DIL_GROUP)
        o, l = dilated_window_attn(q[:, :, sl], k[:, :, sl], v[:, :, sl], win, dil)
        outs.append(o)
        lses.append(l)
    w = jax.nn.softmax(jnp.stack(lses, axis=0), axis=0)
    o = jnp.einsum('gbsh,gbshd->bshd', w, jnp.stack(outs, axis=0).astype(jnp.float32))
    return o.astype(q.dtype).reshape(B, S, WIDTH_A_OUT)

def moba_attn(q, k, v):
    B, S, H, Dh = q.shape
    nB = -(-S // MOBA_BLOCK)
    Sp = nB * MOBA_BLOCK
    padw = ((0, 0), (0, Sp - S), (0, 0), (0, 0))
    qt = jnp.pad(q, padw).transpose(0, 2, 1, 3)
    kt = jnp.pad(k, padw).transpose(0, 2, 1, 3)
    vt = jnp.pad(v, padw).transpose(0, 2, 1, 3)
    kb = kt.reshape(B, H, nB, MOBA_BLOCK, Dh)
    vb = vt.reshape(B, H, nB, MOBA_BLOCK, Dh)
    qpos = jnp.arange(Sp, dtype=jnp.int32)
    qblk = qpos // MOBA_BLOCK
    own = jnp.broadcast_to(qblk[None, None, :, None], (B, H, Sp, 1))
    n_sel = min(MOBA_TOPK, nB - 1)
    if n_sel > 0:
        kmean = jnp.mean(kb.astype(jnp.float32), axis=3)
        gate = jnp.einsum('bhsd,bhnd->bhsn', qt.astype(jnp.float32), kmean)
        past = jnp.arange(nB, dtype=jnp.int32)[None, :] < qblk[:, None]
        _, top_idx = lax.top_k(jnp.where(past, gate, NEG_INF_2), n_sel)
        top_ok = jnp.take_along_axis(jnp.broadcast_to(past, gate.shape), top_idx, axis=-1)
        blk_idx = jnp.concatenate([top_idx.astype(jnp.int32), own], axis=-1)
        blk_ok = jnp.concatenate([top_ok, jnp.ones_like(own, dtype=bool)], axis=-1)
    else:
        blk_idx = own
        blk_ok = jnp.ones_like(own, dtype=bool)
    n_tot = blk_idx.shape[-1]
    nc = Sp // MOBA_Q_CHUNK
    C = MOBA_Q_CHUNK
    q_c = qt.reshape(B, H, nc, C, Dh).transpose(2, 0, 1, 3, 4)
    idx_c = blk_idx.reshape(B, H, nc, C, n_tot).transpose(2, 0, 1, 3, 4)
    ok_c = blk_ok.reshape(B, H, nc, C, n_tot).transpose(2, 0, 1, 3, 4)
    pos_c = qpos.reshape(nc, C)
    bi = jnp.arange(B)[:, None, None, None]
    hi = jnp.arange(H)[None, :, None, None]
    offs = jnp.arange(MOBA_BLOCK, dtype=jnp.int32)

    def chunk(args):
        qc, ic, okc, pc = args
        ks = kb[bi, hi, ic]
        vs = vb[bi, hi, ic]
        s = jnp.einsum('bhcd,bhcnkd->bhcnk', qc, ks).astype(jnp.float32)
        kpos = ic[..., None] * MOBA_BLOCK + offs
        mask = okc[..., None] & (kpos <= pc[None, None, :, None, None])
        s = jnp.where(mask, s, NEG_INF_2).reshape(B, H, C, n_tot * MOBA_BLOCK)
        p = jax.nn.softmax(s, axis=-1).reshape(B, H, C, n_tot, MOBA_BLOCK)
        return jnp.einsum('bhcnk,bhcnkd->bhcd', p.astype(vs.dtype), vs)

    o = lax.map(chunk, (q_c, idx_c, ok_c, pos_c))
    o = o.transpose(1, 2, 0, 3, 4).reshape(B, H, Sp, Dh)
    return o.transpose(0, 2, 1, 3)[:, :S]

def memory_attn(q, mem_n, w_mkv):
    B, S = q.shape[0], q.shape[1]
    M = mem_n.shape[1]
    kv = (mem_n @ w_mkv).reshape(B, M, 2, N_HEADS_M, HEAD_DIM)
    s = jnp.einsum('bshd,bmhd->bhsm', q, kv[:, :, 0]).astype(jnp.float32)
    p = jax.nn.softmax(s, axis=-1)
    o = jnp.einsum('bhsm,bmhd->bshd', p.astype(q.dtype), kv[:, :, 1])
    return o.reshape(B, S, WIDTH_M)

def hybrid_layer(x, mem, pos, g_mix, w_in, w_pa, w_pb, w_pm, w_o, g_mem, w_mkv, g_mlp, w_up, w_down):
    B, S, _ = x.shape
    scale = HEAD_DIM ** -0.5
    h = rms_norm_2(x, g_mix)
    z = h @ w_in
    o1 = 3 * WIDTH_A
    o2 = o1 + 3 * WIDTH_B
    o3 = o2 + WIDTH_M
    qkv_a = z[..., :o1].reshape(B, S, 3, N_HEADS_A, HEAD_DIM)
    qkv_b = z[..., o1:o2].reshape(B, S, 3, N_HEADS_B, HEAD_DIM)
    q_m = z[..., o2:o3].reshape(B, S, N_HEADS_M, HEAD_DIM)
    gates = jax.nn.sigmoid(z[..., o3:].reshape(B, S, N_BRANCH, D_MODEL))
    o_a = dilated_mixer(partial_rope(qkv_a[:, :, 0], pos) * scale,
                        partial_rope(qkv_a[:, :, 1], pos), qkv_a[:, :, 2])
    o_b = moba_attn(partial_rope(qkv_b[:, :, 0], pos) * scale,
                    partial_rope(qkv_b[:, :, 1], pos), qkv_b[:, :, 2]).reshape(B, S, WIDTH_B)
    o_m = memory_attn(q_m * scale, rms_norm_2(mem, g_mem), w_mkv)
    y = (gates[:, :, 0] * (o_a @ w_pa) + gates[:, :, 1] * (o_b @ w_pb)
         + gates[:, :, 2] * (o_m @ w_pm))
    x = x + y @ w_o
    hm = rms_norm_2(x, g_mlp)
    x = x + jnp.square(jax.nn.relu(hm @ w_up)) @ w_down
    return x

def second_inputs(seed: int = 0) -> dict:
    key = jax.random.key(seed)
    ks = jax.random.split(key, 16)

    def nrm(k, shape, fan_in):
        return jax.random.normal(k, shape, jnp.float32) * (fan_in ** -0.5)

    def gain(k, shape):
        return 1.0 + 0.05 * jax.random.normal(k, shape, jnp.float32)

    return {
        'x': jax.random.normal(ks[0], (BATCH, SEQ, D_MODEL), jnp.float32),
        'mem': jax.random.normal(ks[1], (BATCH, N_MEM, D_MODEL), jnp.float32),
        'norm_mix': gain(ks[2], (DEPTH, D_MODEL)),
        'w_in': nrm(ks[3], (DEPTH, D_MODEL, D_IN), D_MODEL),
        'w_proj_a': nrm(ks[4], (DEPTH, WIDTH_A_OUT, D_MODEL), WIDTH_A_OUT),
        'w_proj_b': nrm(ks[5], (DEPTH, WIDTH_B, D_MODEL), WIDTH_B),
        'w_proj_m': nrm(ks[6], (DEPTH, WIDTH_M, D_MODEL), WIDTH_M),
        'w_out': nrm(ks[7], (DEPTH, D_MODEL, D_MODEL), D_MODEL),
        'norm_mem': gain(ks[8], (DEPTH, D_MODEL)),
        'w_mem_kv': nrm(ks[9], (DEPTH, D_MODEL, 2 * WIDTH_M), D_MODEL),
        'norm_mlp': gain(ks[10], (DEPTH, D_MODEL)),
        'w_up': nrm(ks[11], (DEPTH, D_MODEL, D_FF), D_MODEL),
        'w_down': nrm(ks[12], (DEPTH, D_FF, D_MODEL), D_FF),
        'norm_final': gain(ks[13], (D_MODEL,)),
    }

def second_block(x, mem, norm_mix, w_in, w_proj_a, w_proj_b, w_proj_m, w_out, norm_mem, w_mem_kv,
              norm_mlp, w_up, w_down, norm_final):
    pos = jnp.arange(x.shape[1], dtype=jnp.int32)
    for l in range(DEPTH):
        x = hybrid_layer(x, mem, pos, norm_mix[l], w_in[l], w_proj_a[l], w_proj_b[l], w_proj_m[l],
                         w_out[l], norm_mem[l], w_mem_kv[l], norm_mlp[l], w_up[l], w_down[l])
    return rms_norm_2(x, norm_final)


def setup_inputs(seed=0):
    out = dict(first_inputs(seed))
    for name, value in second_inputs(seed + 1).items():
        if name != "x":
            out[name + "_2"] = value
    return out


def reference(
    x, mem, mem_norm_g, w_mem_kv, mem_k_norm_g, cv_attn_norm_g, cv_w_in, cv_b_glu, cv_dw_w,
    cv_dw_b, cv_ln_g, cv_ln_b, cv_memq_norm_g, cv_w_out, cv_ffn_norm_g, cv_w_gate, cv_w_up,
    cv_w_down, sw_attn_norm_g, sw_w_in, sw_q_norm_g, sw_k_norm_g, sw_sinks, sw_memq_norm_g,
    sw_w_out, sw_ffn_norm_g, sw_router, sw_we_gate, sw_we_up, sw_we_down, mem_2, norm_mix_2,
    w_in_2, w_proj_a_2, w_proj_b_2, w_proj_m_2, w_out_2, norm_mem_2, w_mem_kv_2, norm_mlp_2,
    w_up_2, w_down_2, norm_final_2,
):
    x = first_block(
        x, mem, mem_norm_g, w_mem_kv, mem_k_norm_g, cv_attn_norm_g, cv_w_in, cv_b_glu, cv_dw_w,
        cv_dw_b, cv_ln_g, cv_ln_b, cv_memq_norm_g, cv_w_out, cv_ffn_norm_g, cv_w_gate, cv_w_up,
        cv_w_down, sw_attn_norm_g, sw_w_in, sw_q_norm_g, sw_k_norm_g, sw_sinks, sw_memq_norm_g,
        sw_w_out, sw_ffn_norm_g, sw_router, sw_we_gate, sw_we_up, sw_we_down,
    )
    return second_block(
        x, mem_2, norm_mix_2, w_in_2, w_proj_a_2, w_proj_b_2, w_proj_m_2, w_out_2, norm_mem_2,
        w_mem_kv_2, norm_mlp_2, w_up_2, w_down_2, norm_final_2,
    )


_drawn_inputs = setup_inputs


def setup_inputs(seed=0):
    import zlib

    import numpy as np

    out = dict(_drawn_inputs(seed))
    spreads = {}
    factors = {'mem_norm_g': 4.192,
     'mem_k_norm_g': 8.0,
     'cv_memq_norm_g': 8.0,
     'sw_q_norm_g': 3.449,
     'sw_k_norm_g': 3.804,
     'sw_memq_norm_g': 8.0,
     'norm_mix_2': 3.961,
     'norm_mem_2': 8.0}
    for name, (base, spread) in spreads.items():
        noise = np.random.default_rng([zlib.crc32(name.encode()), seed]).standard_normal(out[name].shape)
        drawn = base * np.exp(spread * noise) if base else spread * noise
        out[name] = jnp.asarray(drawn.astype(out[name].dtype))
    for name, factor in factors.items():
        out[name] = (out[name] * factor).astype(out[name].dtype)
    return out
```

```python
import numpy as np
import concourse.bass as bass
from concourse import mybir
from contextlib import ExitStack

F32, F32R, I32 = mybir.dt.float32, mybir.dt.float32r, mybir.dt.int32
ACT, ALU, AX = mybir.ActivationFunctionType, mybir.AluOpType, mybir.AxisListType

P = 128
T = 2
S = T * P
D = 1024
KD = D // P
HD = 64
EPS, LN_EPS = 1e-6, 1e-5
CONV, TAPS = 768, 31
FC = CONV // P
PAD = TAPS - 1
FF1 = 2816
NE, FFE = 8, 3584
KE = FFE // P
FF2 = 4096
MAXJOB = 12
SLOTS = 4
LOOK = 3
QKV2 = 2560
TILES_SMX = 6

FULL = [2, 2, 2, 2]
PANELS_A = 4 + 3 * 4 + 4 + 8 + (FF1 // 256) * 4 + 2 * (FF1 // 256) + 12 + 8
PANELS_M = (FFE // 256) * 4 + 2 * (KE // 2)
PANELS_B = 4 + 11 * 4 + 8 + 8 + 8 * 4 + 2 * 16

PER_JOB = dict(p=PANELS_M, g=16, t=16, n=0, h=0, s=0, a=0, r=0, o=0, va=0, vd=2)
PER_LAYER = dict(p=PANELS_B, g=30, t=26, n=3, h=0, s=16, a=12, r=16, o=6, va=0, vd=53)

SMALL = dict(mem_g=8, cvn=8, cvf=8, swn=8, swf=8, bglu=12, dww=FC * TAPS, dwb=FC, lng=FC, lnb=FC,
             memk=1, cvq=1, swmq=1, swq=1, swk=1, sinks=12, router=KD * NE, norms2=48)
CONST = dict(ident=P, tri=P, ones=P, iota=P, slope=12, low=64, jobs=MAXJOB * NE, experts=MAXJOB * NE,
             dist=2 * S, win=2 * S, dil4=2 * S, dil16=2 * S, causal=2 * S, cosx=T * 16, sinx=T * 16)


def columns(table):
    at, out = 0, {}
    for name, n in table.items():
        out[name] = (at, n)
        at += n
    return out, at


SM, NSM = columns(SMALL)
CO, NCO = columns(CONST)

PAIRS2 = [128 * i for i in range(3)] + [384 + 128 * i for i in range(3)] \
    + [1152 + 128 * i for i in range(3)] + [1536 + 128 * i for i in range(3)] + [2304, 2432]
GROUPS2 = [([0, 1], 'q'), ([2], 'q'), ([3, 4], 'k'), ([5], 'k'), ([6, 7], 'q'), ([8], 'q'),
           ([9, 10], 'k'), ([11], 'k'), ([12, 13], 'q')]


def score_slots(counts):
    plan, owner, at = [], [None] * TILES_SMX, 0
    for i, n in enumerate(counts):
        at = at if at + n <= TILES_SMX else 0
        users = [owner[at + j] for j in range(n) if owner[at + j] is not None]
        plan.append((at, max(users) if users else None, sum(counts[:i])))
        owner[at:at + n] = [i] * n
        at = (at + n) % TILES_SMX
    return plan


def head_stats(stat, i):
    c = 80 + 6 * (i % 4)
    return stat[:, c:c + 2], stat[:, c + 2:c + 4], stat[:, c + 4:c + 6]


def build(nc, d, stop=99):
    ctx = ExitStack()
    with ctx:
        cursor = [16512]

        def sb(name, shape, dt, at=None):
            size = int(np.prod(shape[1:])) * 4
            if at is None:
                at = cursor[0]
                cursor[0] += (size + 31) // 32 * 32
            return nc.alloc_sbuf_tensor_at(name, shape, dt, offset=at)

        raw = sb("raw", [P, SLOTS, 1024], F32)
        whi = sb("whi", [P, SLOTS, 1024], F32R)
        wlo = sb("wlo", [P, SLOTS, 1024], F32R)
        h = sb("h", [P, T, D], F32)
        xhi = sb("xhi", [P, KD, S], F32R)
        xlo = sb("xlo", [P, KD, S], F32R)
        region = cursor[0]
        cursor[0] += 65536
        fhi = sb("fhi", [P, FF2 // P, S], F32R, region)
        flo = sb("flo", [P, FF2 // P, S], F32R, region + 32768)
        mhi = sb("mhi", [P, KE, P], F32R, region)
        mlo = sb("mlo", [P, KE, P], F32R, region + 14336)
        tokhi = sb("tokhi", [P, T, D], F32R, region + 28672)
        toklo = sb("toklo", [P, T, D], F32R, region + 36864)
        outhi = sb("outhi", [P, T, 512], F32R, region + 45056)
        outlo = sb("outlo", [P, T, 512], F32R, region + 49152)
        z = sb("z", [P, T, QKV2], F32, region)
        gates = sb("gates", [P, T, 3 * D], F32, region + 20480)
        chi = sb("chi", [P, KD, S], F32R, region + 45056)
        clo = sb("clo", [P, KD, S], F32R, region + 53248)
        u = sb("u", [P, FC, PAD + S], F32, region + 20480)
        cacc = sb("cacc", [P, FC, S], F32, region + 20480 + 6912)
        ctok = sb("ctok", [P, T, CONV], F32, region + 20480 + 13056)

        hn = sb("hn", [P, T, D], F32)
        mbuf = sb("mbuf", [P, T, D], F32)
        mkv = sb("mkv", [P, T, 512], F32)
        mkT = sb("mkT", [P, 2, S], F32)
        qkT = sb("qkT", [P, 14, S], F32)
        SMX = sb("SMX", [P, TILES_SMX, T, S], F32)
        scratch = SMX[:, :, :, :].rearrange("p a c d -> p (a c d)")
        PT = sb("PT", [P, 2, 2 * S], F32)
        sg = sb("sg", [P, 2, 512], F32)
        small = sb("small", [P, NSM], F32)
        const = sb("const", [P, NCO], F32)
        stat = sb("stat", [P, 160], F32)
        halfneg = sb("halfneg", [P, 1], F32)
        n2 = sb("n2", [P, 24], F32)
        jobpos = sb("jobpos", [P, T, MAXJOB], F32, region + 61952)
        jobgate = sb("jobgate", [P, T, MAXJOB], F32, region + 62048)
        jobcur = sb("jobcur", [P, 2, T], F32)
        sel = sb("sel", [P, T, P], F32R, region + 53248)
        selT = sb("selT", [P, T, P], F32R, region + 54272)
        rhi = sb("rhi", [P, KD * NE], F32R, region + 61440)
        rlo = sb("rlo", [P, KD * NE], F32R, region + 61696)
        tab = sb("tab", [1, 1 + MAXJOB], I32)
        assert cursor[0] <= 229344, cursor[0]

        def sp(name, a=0, n=None):
            c, m = SM[name]
            return small[:, c + a:c + a + (m if n is None else n)]

        def co(name, a=0, n=None):
            c, m = CO[name]
            return const[:, c + a:c + a + (m if n is None else n)]

        ident = co("ident")
        mask = {k: co(k) for k in ("dist", "win", "dil4", "dil16", "causal")}

        L = [ctx.enter_context(nc.psum_tensor(f"L{i}", [P, 512], F32)) for i in range(4)]
        SC = [ctx.enter_context(nc.psum_tensor(f"SC{i}", [P, 512], F32)) for i in range(2)]
        TB = [ctx.enter_context(nc.psum_tensor(f"TB{i}", [P, 512], F32)) for i in range(2)]

        def sem(name):
            return ctx.enter_context(nc.semaphore(name))

        class Signals:
            def __init__(self, q):
                self.raw = [sem(f"{q}raw{i}") for i in range(SLOTS)]
                self.hi = sem(q + "hi")
                self.lo = sem(q + "lo")
                self.used = sem(q + "used")
                self.free = sem(q + "free")
                self.tdone = sem(q + "tdone")
                self.thi = sem(q + "thi")
                self.tfree = sem(q + "tfree")
                self.nss = sem(q + "nss")
                self.nms = sem(q + "nms")
                self.nr = sem(q + "nr")
                self.nhn = sem(q + "nhn")
                self.hsq = sem(q + "hsq")
                self.hms = sem(q + "hms")
                self.hr = sem(q + "hr")
                self.zrdy = sem(q + "zrdy")
                self.sdone = sem(q + "sdone")
                self.sfree = sem(q + "sfree")
                self.mx = sem(q + "mx")
                self.ex = sem(q + "ex")
                self.pr = sem(q + "pr")
                self.rdone = sem(q + "rdone")
                self.rcopy = sem(q + "rcopy")
                self.pv = sem(q + "pv")
                self.ohi = sem(q + "ohi")
                self.ofree = sem(q + "ofree")
                self.va = sem(q + "va")
                self.vd = sem(q + "vd")

        panels_a = {1: 28, 2: 94, 3: 94}.get(stop, PANELS_A)
        A, B = Signals("a_"), Signals("b_")
        s_gf = sem("s_gf")
        s_in = [sem(f"s_in{i}") for i in range(4)]
        s_mem2 = sem("s_mem2")
        s_out = sem("s_out")
        s_pre = sem("s_pre")
        s_ev = sem("s_ev")
        s_sig = sem("s_sig")
        s_conv = sem("s_conv")
        s_ln = sem("s_ln")
        s_lnp = sem("s_lnp")
        s_silu = sem("s_silu")
        s_act = sem("s_act")
        s_fhi = sem("s_fhi")
        s_frdy = sem("s_frdy")
        s_h = sem("s_h")
        s_tok = sem("s_tok")
        s_tokl = sem("s_tokl")
        s_rt = sem("s_rt")
        s_rv = sem("s_rv")
        s_ra = sem("s_ra")
        s_tab = sem("s_tab")
        s_sel = sem("s_sel")
        s_gat = sem("s_gat")
        s_xhi = sem("s_xhi")
        s_xj = sem("s_xj")
        s_scat = sem("s_scat")
        s_oh = sem("s_oh")
        s_ol = sem("s_ol")
        s_u = [sem("s_sig2"), sem("s_sq2")]
        s_r2 = sem("s_r2")
        s_q2 = sem("s_q2")
        s_h2 = sem("s_h2")
        s_l2 = sem("s_l2")
        s_z2 = sem("s_z2")
        s_g2 = sem("s_g2")
        s_y2 = sem("s_y2")
        s_res = sem("s_res")
        s_par = sem("s_par")

        class Walk:
            def __init__(self, e, s, chain=None):
                self.e, self.s, self.chain = e, s, chain
                self.key = "va" if chain is s.va else "vd"
                self.n = dict.fromkeys(PER_JOB, 0)
                self.split = 0
                self.it, self.per = None, None

            def at(self, kind, plus=0):
                v = self.n[kind] + plus
                return v if self.it is None else self.it * self.per[kind] + v

            def loop(self, it, per):
                self.it, self.per, self.begin = it, per, dict(self.n)

            def after(self, turns):
                self.it, self.n = turns, dict(self.begin)

            def end(self, kinds):
                for k in kinds:
                    got = self.n[k] - self.begin[k]
                    assert got == self.per[k], (k, got, self.per[k])

            def mark(self, ins):
                self.n[self.key] += 1
                ins.then_inc(self.chain, 1)
                return self.at(self.key)

            def need(self, value):
                self.e.wait_ge(self.chain, value)

            def link(self, ins):
                self.need(self.mark(ins))

        block = ctx.enter_context(nc.Block())

        @block.sync
        def _(e):
            def panels(s, source, n, first=0, it=None, per=0):
                for i in range(n):
                    p = first + i
                    v = p + 1 if it is None else it * per + (p + 1)
                    e.wait_ge(s.lo, v)
                    e.dma_start(raw[:, p % SLOTS, :], source(i)).then_inc(s.raw[p % SLOTS], 16)

            e.dma_start(mbuf[:, :, :], d["mem"].rearrange("(t p) n -> p t n", p=P)).then_inc(s_in[3], 16)
            first = 8
            panels(A, lambda i: d["w1"][i], first)
            e.wait_ge(A.nhn, 1)
            e.dma_start(mbuf[:, :, :], d["mem2"].rearrange("(t p) n -> p t n", p=P)).then_inc(s_mem2, 16)
            rest = panels_a - first
            turns = rest // SLOTS
            with e.Fori(0, turns) as k:
                for i in range(SLOTS):
                    p = first + i
                    e.wait_ge(A.lo, k * SLOTS + (p + 1))
                    e.dma_start(raw[:, p % SLOTS, :], d["w1"][bass.ds(k * SLOTS + p, 1)].rearrange("a p n -> p (a n)")
                                ).then_inc(A.raw[p % SLOTS], 16)
            done = first + turns * SLOTS
            panels(A, lambda i: d["w1"][done + i], panels_a - done, done)
            hout = d["out"].rearrange("(t p) n -> p t n", p=P)
            if stop < 6:
                e.wait_ge(s_h, {1: 2, 2: 4, 3: 4}.get(stop, 6))
                e.dma_start(hout, h[:, :, :]).then_inc(s_out, 16)
                e.wait_ge(s_out, 16)
                return
            e.wait_ge(s_tab, 1)
            jobs = e.value_load(tab[0:1, 0:1], min_val=1, max_val=MAXJOB - 1)

            def expert_panel(expert, panel, slot, split):
                e.wait_ge(A.lo, split)
                e.dma_start(raw[:, slot, :], d["wm"][bass.ds(expert * PANELS_M + panel, 1)].rearrange("a p n -> p (a n)")
                            ).then_inc(A.raw[slot], 16)

            slots = [(PANELS_A + i) % SLOTS for i in range(SLOTS)]
            expert = e.value_load(tab[0:1, 1:2], min_val=0, max_val=NE - 1)
            for i in range(SLOTS):
                expert_panel(expert, i, slots[i], PANELS_A + i + 1)
            with e.Fori(0, jobs) as j:
                expert = e.value_load(tab[0:1, bass.ds(j + 1, 1)], min_val=0, max_val=NE - 1)
                with e.Fori(0, PANELS_M // SLOTS - 1) as k:
                    for i in range(SLOTS):
                        expert_panel(expert, k * SLOTS + (SLOTS + i), slots[i],
                                     j * PANELS_M + k * SLOTS + (PANELS_A + SLOTS + i + 1))
                follower = e.value_load(tab[0:1, bass.ds(j + 2, 1)], min_val=0, max_val=NE - 1)
                for i in range(SLOTS):
                    expert_panel(follower, i, slots[i], j * PANELS_M + (PANELS_A + PANELS_M + i + 1))
            if stop < 7:
                e.wait_ge(s_h, jobs * 2 + 8)
                e.dma_start(hout, h[:, :, :]).then_inc(s_out, 16)
                e.wait_ge(s_out, 16)
                return
            with e.Fori(0, 2 * PANELS_B // SLOTS) as k:
                for i in range(SLOTS):
                    e.wait_ge(B.lo, k * SLOTS + (i + 1))
                    e.dma_start(raw[:, i, :], d["w2"][bass.ds(k * SLOTS + i, 1)].rearrange("a p n -> p (a n)")
                                ).then_inc(B.raw[i], 16)
            e.wait_ge(B.nhn, 4)
            e.dma_start(mbuf[:, 0, :], d["gfin"]).then_inc(s_gf, 16)
            e.wait_ge(B.nhn, 7)
            e.dma_start(hout, hn[:, :, :]).then_inc(s_out, 16)
            e.wait_ge(s_out, 16)

        @block.gpsimd
        def _(e):
            e.memset(halfneg[:, :], -0.5).then_inc(s_lnp, 1)
            e.wait_ge(s_lnp, 1)

            def power(ready, v, src, n, done):
                e.wait_ge(ready, v)
                e.tensor_tensor(src, src, halfneg[:, 0:1].to_broadcast([P, n]), ALU.pow).then_inc(done, 1)

            def row(w):
                power(w.s.nms, w.at("n", 1), stat[:, 0:T], T, w.s.nr)
                w.n["n"] += 1

            def heads(w, nh):
                power(w.s.hms, w.at("h", 1), stat[:, 32:32 + T * nh], T * nh, w.s.hr)
                w.n["h"] += 1

            w = Walk(e, A)
            row(w)
            heads(w, 4)
            row(w)
            heads(w, 4)
            power(s_ln, 4, stat[:, 8:8 + T], T, s_lnp)
            if stop < 2:
                return
            row(w)
            if stop < 4:
                return
            row(w)
            heads(w, 20)
            if stop < 6:
                return
            row(w)
            if stop < 7:
                return
            w = Walk(e, B)
            with e.Fori(0, 2) as l:
                w.loop(l, PER_LAYER)
                for _ in range(3):
                    row(w)
                w.end("n")
            w.it, w.n["n"] = None, 6
            row(w)

        @block.scalar
        def _(e):
            act = nc.scalar.activation

            def split_to(w, target):
                while w.split < target:
                    p = w.split
                    w.split += 1
                    base = 16 * (p // SLOTS + 1)
                    e.wait_ge(w.s.raw[p % SLOTS], base if w.it is None else w.it * (4 * w.per["p"]) + base)
                    q = p + 1
                    e.wait_ge(w.s.used, q if w.it is None else w.it * w.per["p"] + q)
                    act(whi[:, p % SLOTS, :], raw[:, p % SLOTS, :], ACT.Copy).then_inc(w.s.hi, 1)

            def chunk(w, np_, last):
                w.n["p"] += np_
                split_to(w, min(w.n["p"] + LOOK, last))
                w.n["g"] += 1

            def complete(w):
                e.wait_ge(w.s.used, w.at("p", SLOTS))

            def norm(w, src, ready, gain, last):
                e.wait_ge(*ready)
                e.wait_ge(w.s.tfree, w.at("t", 2))
                for t in range(T):
                    i = act(hn[:, t, :], src[:, t, :], ACT.Square, accum_out=stat[:, t:t + 1])
                i.then_inc(w.s.nss, 1)
                w.n["n"] += 1
                turned(w, gain)

            def turned(w, gain):
                e.wait_ge(w.s.used, w.at("p", SLOTS))
                for q in range(4):
                    e.wait_ge(w.s.tdone, w.at("t", 1))
                    bank = TB[w.n["t"] % 2]
                    for kk in range(2):
                        k = 2 * q + kk
                        i = act(xhi[:, k, :], bank[:, kk * S:(kk + 1) * S], ACT.Copy,
                                scale=1.0 if gain is None else gain(k))
                    i.then_inc(w.s.thi, 1)
                    w.n["t"] += 1

            def head_squares(w, parts):
                e.wait_ge(*parts[0])
                for src, dst in parts[1]:
                    i = act(dst, src, ACT.Square)
                i.then_inc(w.s.hsq, 1)
                w.n["h"] += 1

            def turned_heads(w, groups):
                for dst, n, scale in groups:
                    e.wait_ge(w.s.tdone, w.at("t", 1))
                    bank = TB[w.n["t"] % 2][:, 0:n * S].rearrange("p (a s) -> p a s", s=S)
                    act(dst[:, :, 0:P], bank[:, :, 0:P], ACT.Copy, scale=scale).then_inc(w.s.thi, 1)
                    w.n["t"] += 1

            def attention(w, heads):
                plan = score_slots([len(x[0]) for x in heads])

                def exps(i):
                    parts, sink, _ = heads[i]
                    slot, n = plan[i][0], len(parts)
                    neg_max, total, sunk = head_stats(stat, i)
                    e.wait_ge(w.s.mx, w.at("a", i + 1))
                    for t in range(T):
                        x = SMX[:, slot:slot + n, t, :]
                        ins = act(x, x, ACT.Exp, bias=neg_max[:, t:t + 1], accum_out=total[:, t:t + 1])
                    if sink is not None:
                        ins = act(sunk, neg_max, ACT.Exp, bias=sink)
                    ins.then_inc(w.s.ex, 1)

                def copies(i):
                    for _ in heads[i][0]:
                        e.wait_ge(w.s.rdone, w.at("r", 1))
                        e.wait_ge(w.s.pv, w.at("r", 1))
                        r = w.n["r"]
                        act(PT[:, r % 2, :], TB[r % 2][:, :], ACT.Copy).then_inc(w.s.rcopy, 1)
                        w.n["r"] += 1

                r0 = w.n["r"]

                def pair_out(i):
                    done = r0 - w.n["r"] + plan[i][2] + len(heads[i][0])
                    e.wait_ge(w.s.pv, w.at("r", done + 2))
                    act(chi[:, heads[i][2], :], L[w.n["o"] % 2][:, 0:S], ACT.Copy).then_inc(w.s.ohi, 1)
                    w.n["o"] += 1

                exps(0)
                exps(1)
                for i in range(len(heads)):
                    copies(i)
                    if i + 2 < len(heads):
                        exps(i + 2)
                    if i >= 1 and heads[i - 1][2] is not None:
                        pair_out(i - 1)
                pair_out(len(heads) - 1)
                w.n["a"] += len(heads)

            e.dma_start(const[:, :], d["const"]).then_inc(s_in[0], 16)
            e.dma_start(small[:, :], d["small"]).then_inc(s_in[1], 16)
            e.dma_start(h[:, :, :], d["x"].rearrange("(t p) n -> p t n", p=P)).then_inc(s_in[2], 16)

            w = Walk(e, A, A.va)
            last = panels_a
            e.wait_ge(s_in[1], 16)
            norm(w, mbuf, (s_in[3], 16), lambda k: sp("mem_g", k, 1), last)
            chunk(w, 4, last)
            e.wait_ge(s_ev, 1)
            head_squares(w, ((s_ev, 1), [(mkv[:, :, 0:256], scratch[:, 0:512].rearrange("p (t n) -> p t n", t=T))]))
            norm_ready = (s_in[2], 16)
            turned_heads(w, [(mkT, 2, sp("memk"))])
            norm(w, h, norm_ready, lambda k: sp("cvn", k, 1), last)
            for c in range(3):
                chunk(w, 4, last)
                complete(w)
                g = w.n["g"] - 1
                e.wait_ge(s_ev, 1 + max(c, 0))
                for f in range(2):
                    i = act(sg[:, 0, f * S:(f + 1) * S], L[2 * (g % 2) + 1][:, f * S:(f + 1) * S], ACT.Sigmoid,
                            bias=sp("bglu", FC + 2 * c + f, 1))
                i.then_inc(s_sig, 1)
            chunk(w, 4, last)
            head_squares(w, ((s_ev, 5), [(z[:, :, 0:256], scratch[:, 0:512].rearrange("p (t n) -> p t n", t=T))]))
            turned_heads(w, [(qkT[:, 0:2, :], 2, sp("cvq"))])
            for q in range(3):
                e.wait_ge(w.s.tdone, w.at("t", 1))
                act(ctok[:, 0, q * S:(q + 1) * S], TB[w.n["t"] % 2][:, 0:S], ACT.Copy).then_inc(w.s.thi, 1)
                w.n["t"] += 1
            e.wait_ge(w.s.tfree, w.at("t", 2))
            for t in range(T):
                i = act(hn[:, t, 0:CONV], ctok[:, t, :], ACT.Copy, accum_out=stat[:, 8 + t:9 + t])
            i.then_inc(s_ln, 1)
            e.wait_ge(s_ln, 2)
            for t in range(T):
                i = act(hn[:, t, 0:CONV], ctok[:, t, :], ACT.Square, accum_out=stat[:, 8 + t:9 + t])
            i.then_inc(s_ln, 1)
            for q in range(3):
                e.wait_ge(w.s.tdone, w.at("t", 1))
                for kk in range(2):
                    k = 2 * q + kk
                    m = w.mark(act(hn[:, 0, kk * S:(kk + 1) * S], TB[w.n["t"] % 2][:, kk * S:(kk + 1) * S], ACT.Silu,
                                   scale=sp("lng", k, 1), bias=sp("lnb", k, 1)))
                w.need(m)
                act(chi[:, 2 * q:2 * q + 2, :], hn[:, 0, 0:512].rearrange("p (a s) -> p a s", s=S), ACT.Copy
                    ).then_inc(w.s.thi, 1)
                w.n["t"] += 1
                e.wait_ge(w.s.tfree, w.at("t", 2))
            attention(w, [([0], None, None), ([0], None, 6), ([0], None, None), ([0], None, 7)])
            for c in range(2):
                chunk(w, 4, last)
            if stop < 2:
                return
            norm(w, h, (s_h, 2), lambda k: sp("cvf", k, 1), last)

            for c in range(FF1 // 256):
                chunk(w, 4, last)
                complete(w)
                g = w.n["g"] - 1
                if c >= 2:
                    e.wait_ge(s_frdy, c - 1)
                act(sg[:, c % 2, :], L[2 * (g % 2)][:, :], ACT.Silu).then_inc(s_silu, 1)
                e.wait_ge(s_act, c + 1)
                act(fhi[:, 2 * c:2 * c + 2, :], sg[:, c % 2, :].rearrange("p (a s) -> p a s", s=S), ACT.Copy
                    ).then_inc(s_fhi, 1)
            for c in range(2):
                chunk(w, FF1 // 256, last)
            if stop < 4:
                return
            norm(w, h, (s_h, 4), lambda k: sp("swn", k, 1), last)
            for c in range(3):
                chunk(w, 4, last)
            head_squares(w, ((s_ev, 8), [
                (z[:, :, 0:1024], scratch[:, 0:2048].rearrange("p (t n) -> p t n", t=T)),
                (z[:, :, 1280:1536], scratch[:, 2048:2560].rearrange("p (t n) -> p t n", t=T))]))
            turned_heads(w, [(qkT[:, 2 * i:2 * i + 2, :], 2, sp("swq")) for i in range(3)]
                         + [(qkT[:, 6:8, :], 2, sp("swk")), (qkT[:, 8:10, :], 2, sp("swmq"))])
            attention(w, [([0], sp("sinks", i, 1) if i < 12 else None, i // 2 if i % 2 else None) for i in range(16)])
            for c in range(2):
                chunk(w, 4, last)
            if stop < 6:
                return
            norm(w, h, (s_h, 6), lambda k: sp("swf", k, 1), last)
            act(tokhi[:, :, :], hn[:, :, :], ACT.Copy).then_inc(s_tok, 1)
            e.wait_ge(s_rv, 2)
            act(stat[:, 128:144], stat[:, 128:144], ACT.Exp).then_inc(s_ra, 1)
            e.wait_ge(s_tab, 1)
            jobs = e.value_load(tab[0:1, 0:1], min_val=1, max_val=MAXJOB - 1)

            def gathered_hi(n):
                e.wait_ge(s_gat, n)
                for k in range(KD):
                    i = act(xhi[:, k, 0:P], SC[k // 4][:, (k % 4) * P:(k % 4 + 1) * P], ACT.Copy, scale=sp("swf", k, 1))
                i.then_inc(s_xhi, 1)

            def hidden_hi(c):
                e.wait_ge(w.s.tdone, w.at("t", 1))
                act(mhi[:, 2 * c:2 * c + 2, :], TB[w.n["t"] % 2][:, 0:S].rearrange("p (a s) -> p a s", s=P),
                    ACT.Copy).then_inc(w.s.thi, 1)
                w.n["t"] += 1

            last = 1 << 30
            gathered_hi(1)
            split_to(w, w.n["p"] + LOOK)
            with e.Fori(0, jobs) as j:
                w.loop(j, PER_JOB)
                for c in range(FFE // 256):
                    chunk(w, 4, last)
                    complete(w)
                    g = w.n["g"] - 1
                    e.wait_ge(s_act, j * 14 + (FF1 // 256 + max(c - 1, 0)))
                    act(sg[:, c % 2, 0:256], L[2 * (g % 2)][:, 0:256], ACT.Silu).then_inc(s_silu, 1)
                    if c >= 1:
                        hidden_hi(c - 1)
                    if c == 3:
                        for t in range(T):
                            e.wait_ge(w.s.tdone, w.at("t", 1))
                            act(selT[:, t, 0:HD], TB[w.n["t"] % 2][:, 0:HD], ACT.Copy).then_inc(w.s.thi, 1)
                            w.n["t"] += 1
                split_to(w, w.n["p"] + 6)
                hidden_hi(FFE // 256 - 1)
                for c in range(2):
                    if c == 1:
                        gathered_hi(j + 2)
                    chunk(w, KE // 2, last)
                    complete(w)
                    g = w.n["g"] - 1
                    act(outhi[:, c, :], L[2 * (g % 2)][:, :], ACT.Copy).then_inc(s_oh, 1)
                w.end("pgt")
            w.after(jobs)
            w.split = w.begin["p"] + LOOK
            split_to(w, w.n["p"] + SLOTS)
            if stop < 7:
                return

            w = Walk(e, B, B.va)
            with e.Fori(0, 2) as l:
                w.loop(l, PER_LAYER)
                last = PANELS_B
                split_to(w, LOOK)
                e.wait_ge(s_par, l + 1)
                norm(w, mbuf, (s_mem2, 16), lambda k: n2[:, k:k + 1], last)
                chunk(w, 4, last)
                turned_heads(w, [(mkT, 2, 1.0)])
                e.wait_ge(s_h, jobs * 2 + 8)
                norm(w, h, (s_res, l * 4 + 0 + 4), lambda k: n2[:, 8 + k:9 + k], last)
                for c in range(11):
                    chunk(w, 4, last)
                    if c >= 5:
                        complete(w)
                        g = w.n["g"] - 1
                        e.wait_ge(w.s.free, w.at("g", 1))
                        for t in range(T):
                            i = act(gates[:, t, (c - 5) * 512:(c - 4) * 512], L[2 * (g % 2) + t][:, :], ACT.Sigmoid)
                        i.then_inc(w.s.free, 1)
                turned_heads(w, [(qkT[:, a[0]:a[-1] + 1, :], len(a), 0.125 if kind == "q" else 1.0)
                                 for a, kind in GROUPS2])
                attention(w, [([0, 1, 2], None, None), ([0, 1, 2], None, 0)]
                          + [([0], None, 1 + i // 2 if i % 2 else None) for i in range(10)])
                for c in range(6):
                    chunk(w, [1, 2, 1][c % 3], last)
                turned(w, None)
                for c in range(2):
                    chunk(w, 4, last)
                norm(w, h, (s_res, l * 4 + 2 + 4), lambda k: n2[:, 16 + k:17 + k], last)
                for c in range(8):
                    chunk(w, 4, last)
                    complete(w)
                    g = w.n["g"] - 1
                    for b in range(2):
                        n = 2 * c + b
                        if n >= 2:
                            e.wait_ge(s_l2, l * 16 + n - 1)
                        act(sg[:, b, :], L[2 * (g % 2) + b][:, :], ACT.Relu).then_inc(s_r2, 1)
                    for b in range(2):
                        n = 2 * c + b
                        e.wait_ge(s_q2, l * 16 + n + 1)
                        act(fhi[:, 4 * c + 2 * b:4 * c + 2 * b + 2, :],
                            sg[:, b, :].rearrange("p (a s) -> p a s", s=S), ACT.Copy).then_inc(s_h2, 1)
                for c in range(2):
                    chunk(w, 16, last)
                w.end("pgtnaro")
            w.it = None
            e.wait_ge(s_res, 12)
            for t in range(T):
                i = act(hn[:, t, :], h[:, t, :], ACT.Square, accum_out=stat[:, t:t + 1])
            i.then_inc(B.nss, 1)

        @block.vector
        def _(e):
            v = nc.vector

            def split_to(w, target):
                while w.split < target:
                    p = w.split
                    w.split += 1
                    q = p + 1
                    e.wait_ge(w.s.hi, q if w.it is None else w.it * w.per["p"] + q)
                    v.tensor_tensor(wlo[:, p % SLOTS, :], raw[:, p % SLOTS, :], whi[:, p % SLOTS, :].bitcast(F32),
                                    ALU.subtract).then_inc(w.s.lo, 1)

            def chunk(w, np_, last):
                w.n["p"] += np_
                split_to(w, min(w.n["p"] + LOOK, last))
                e.wait_ge(w.s.used, w.at("p", SLOTS))
                e.wait_ge(w.s.free, w.at("g", 2))
                w.n["g"] += 1
                return L[2 * ((w.n["g"] - 1) % 2)], L[2 * ((w.n["g"] - 1) % 2) + 1]

            def norm(w, gain):
                e.wait_ge(w.s.nss, w.at("n", 1))
                v.tensor_scalar(stat[:, 0:T], stat[:, 0:T], 1.0 / D, EPS, ALU.mult, ALU.add).then_inc(w.s.nms, 1)
                e.wait_ge(w.s.nr, w.at("n", 1))

            def norm_rows(w, src, gain):
                norm(w, gain)
                for t in range(T):
                    i = v.tensor_scalar(hn[:, t, :], src[:, t, :], stat[:, t:t + 1], None, ALU.mult)
                i.then_inc(w.s.nhn, 1)
                w.n["n"] += 1
                turned(w, gain)

            def turned(w, gain):
                for q in range(4):
                    e.wait_ge(w.s.thi, w.at("t", 1))
                    bank = TB[w.n["t"] % 2]
                    for kk in range(2):
                        k = 2 * q + kk
                        i = v.scalar_tensor_tensor(xlo[:, k, :], bank[:, kk * S:(kk + 1) * S],
                                                   1.0 if gain is None else gain(k), xhi[:, k, :].bitcast(F32),
                                                   ALU.mult, ALU.subtract)
                    i.then_inc(w.s.tfree, 1)
                    w.n["t"] += 1

            def head_norm(w, blocks, nh):
                e.wait_ge(w.s.hsq, w.at("h", 1))
                for sq, _, c, n in blocks:
                    for t in range(T):
                        m = w.mark(v.reduce_sum(stat[:, c + t * n:c + (t + 1) * n],
                                                sq[:, t, :].rearrange("p (a k) -> p a k", k=HD), axis=AX.X))
                w.need(m)
                v.tensor_scalar(stat[:, 32:32 + T * nh], stat[:, 32:32 + T * nh], 1.0 / HD, EPS, ALU.mult, ALU.add
                                ).then_inc(w.s.hms, 1)
                e.wait_ge(w.s.hr, w.at("h", 1))
                for _, rows, c, n in blocks:
                    for t in range(T):
                        x = rows[:, t, :].rearrange("p (a k) -> p a k", k=HD)
                        r = stat[:, c + t * n:c + (t + 1) * n].unsqueeze(2).to_broadcast([P, n, HD])
                        i = v.tensor_tensor(x, x, r, ALU.mult)
                i.then_inc(w.s.zrdy, 1)
                w.n["h"] += 1

            def turned_heads(w, groups):
                for dst, n, scale in groups:
                    e.wait_ge(w.s.thi, w.at("t", 1))
                    bank = TB[w.n["t"] % 2][:, 0:n * S].rearrange("p (a s) -> p a s", s=S)
                    v.tensor_scalar(dst[:, :, P:S], bank[:, :, P:S], scale, None, ALU.mult).then_inc(w.s.tfree, 1)
                    w.n["t"] += 1

            def attention(w, heads):
                plan = score_slots([len(x[0]) for x in heads])

                def scores(i):
                    masks, sink, _, slope = heads[i]
                    slot, user, _ = plan[i]
                    if user is not None:
                        e.wait_ge(w.s.rdone, w.at("r", plan[user][2] + len(heads[user][0])))
                    for j, m in enumerate(masks):
                        e.wait_ge(w.s.sdone, w.at("s", 1))
                        src, dst = SC[w.n["s"] % 2][:, :], SMX[:, slot + j].rearrange("p t s -> p (t s)")
                        if slope is not None:
                            ins = v.scalar_tensor_tensor(dst, m, slope, src, ALU.mult, ALU.add)
                        elif m is not None:
                            ins = v.tensor_tensor(dst, src, m, ALU.add)
                        else:
                            ins = v.tensor_copy(dst, src)
                        ins.then_inc(w.s.sfree, 1)
                        w.n["s"] += 1
                    e.wait_ge(w.s.sfree, w.at("s", 2))
                    x = SMX[:, slot:slot + len(masks)].rearrange("p r t s -> p t r s")
                    mx = head_stats(stat, i)[0]
                    if sink is None:
                        v.tensor_reduce(mx, x, axis=AX.XY, op=ALU.max, negate=True).then_inc(w.s.mx, 1)
                    else:
                        w.link(v.tensor_reduce(mx, x, axis=AX.XY, op=ALU.max))
                        v.tensor_scalar(mx, mx, sink, -1.0, ALU.max, ALU.mult).then_inc(w.s.mx, 1)

                def probs(i):
                    masks, sink, _, _ = heads[i]
                    slot = plan[i][0]
                    _, den, sunk = head_stats(stat, i)
                    e.wait_ge(w.s.ex, w.at("a", i + 1))
                    if sink is not None:
                        w.link(v.tensor_tensor(den, den, sunk, ALU.add))
                    w.link(v.reciprocal(den, den))
                    for t in range(T):
                        x = SMX[:, slot:slot + len(masks), t, :]
                        ins = v.tensor_scalar(x, x, den[:, t:t + 1], None, ALU.mult)
                    ins.then_inc(w.s.pr, 1)

                def pair_out(tile):
                    e.wait_ge(w.s.ohi, w.at("o", 1))
                    v.tensor_tensor(clo[:, tile, :], L[w.n["o"] % 2][:, 0:S], chi[:, tile, :].bitcast(F32), ALU.subtract
                                    ).then_inc(w.s.ofree, 1)
                    w.n["o"] += 1

                scores(0)
                scores(1)
                for i in range(len(heads)):
                    probs(i)
                    if i + 2 < len(heads):
                        scores(i + 2)
                    if i >= 2 and heads[i - 2][2] is not None:
                        pair_out(heads[i - 2][2])
                pair_out(heads[-1][2])
                w.n["r"] += sum(len(x[0]) for x in heads)
                w.n["a"] += len(heads)

            def add_rows(w, banks, n, done):
                for t in range(T):
                    x = h[:, t, n * 512:(n + 1) * 512]
                    i = v.tensor_tensor(x, banks[t][:, :], x, ALU.add)
                w.need(w.mark(i))
                e.sem_inc(w.s.free)
                e.sem_inc(done)

            w = Walk(e, A, A.vd)
            e.drain().then_inc(A.lo, SLOTS)
            e.drain().then_inc(A.free, 2)
            e.drain().then_inc(A.tfree, 2)
            e.drain().then_inc(A.sfree, 2)
            e.drain().then_inc(A.ofree, 2)
            v.memset(u[:, :, 0:PAD], 0.0).then_inc(s_pre, 1)
            e.wait_ge(s_in[0], 16)
            e.wait_ge(s_in[1], 16)
            for name in ("cvq", "swq", "swmq"):
                v.tensor_scalar(sp(name), sp(name), HD ** -0.5, None, ALU.mult).then_inc(s_pre, 1)
            v.tensor_copy(rhi[:, :], sp("router")).then_inc(s_pre, 1)
            e.wait_ge(s_pre, 5)
            v.tensor_tensor(rlo[:, :], sp("router"), rhi[:, :].bitcast(F32), ALU.subtract).then_inc(s_pre, 1)
            last = panels_a
            norm_rows(w, mbuf, lambda k: sp("mem_g", k, 1))
            banks = chunk(w, 4, last)
            for t in range(T):
                w.link(v.tensor_copy(mkv[:, t, :], banks[t][:, :]))
            e.sem_inc(A.free)
            e.sem_inc(s_ev)
            head_norm(w, [(scratch[:, 0:512].rearrange("p (t n) -> p t n", t=T), mkv[:, :, 0:256], 32, 4)], 4)
            turned_heads(w, [(mkT, 2, sp("memk"))])
            norm_rows(w, h, lambda k: sp("cvn", k, 1))
            for c in range(3):
                banks = chunk(w, 4, last)
                e.wait_ge(s_sig, c + 1)
                for f in range(2):
                    i = v.scalar_tensor_tensor(u[:, 2 * c + f, PAD:PAD + S], banks[0][:, f * S:(f + 1) * S],
                                               sp("bglu", 2 * c + f, 1), sg[:, 0, f * S:(f + 1) * S], ALU.add, ALU.mult)
                w.link(i)
                e.sem_inc(A.free)
                e.sem_inc(s_ev)
                marks = [None, None]
                for tap in range(TAPS):
                    for f in range(2):
                        k = 2 * c + f
                        tapw = sp("dww", k * TAPS + tap, 1)
                        if tap == 0:
                            ins = v.tensor_scalar(cacc[:, k, :], u[:, k, 0:S], tapw, sp("dwb", k, 1), ALU.mult, ALU.add)
                        else:
                            w.need(marks[f])
                            ins = v.scalar_tensor_tensor(cacc[:, k, :], u[:, k, tap:tap + S], tapw, cacc[:, k, :],
                                                         ALU.mult, ALU.add)
                        if tap < TAPS - 1:
                            marks[f] = w.mark(ins)
                        elif f == 0:
                            w.mark(ins)
                        else:
                            ins.then_inc(s_conv, 1)
            banks = chunk(w, 4, last)
            for t in range(T):
                w.link(v.tensor_copy(z[:, t, 0:256], banks[t][:, 0:256]))
            e.sem_inc(A.free)
            e.sem_inc(s_ev)
            head_norm(w, [(scratch[:, 0:512].rearrange("p (t n) -> p t n", t=T), z[:, :, 0:256], 32, 4)], 4)
            turned_heads(w, [(qkT[:, 0:2, :], 2, sp("cvq"))])
            for q in range(3):
                e.wait_ge(w.s.thi, w.at("t", 1))
                v.tensor_copy(ctok[:, 1, q * S:(q + 1) * S], TB[w.n["t"] % 2][:, S:2 * S]).then_inc(w.s.tfree, 1)
                w.n["t"] += 1
            e.wait_ge(s_ln, 1)
            w.link(v.tensor_scalar(stat[:, 8:8 + T], stat[:, 8:8 + T], 1.0 / CONV, None, ALU.mult))
            for t in range(T):
                i = v.tensor_scalar(ctok[:, t, :], ctok[:, t, :], stat[:, 8 + t:9 + t], None, ALU.subtract)
            i.then_inc(s_ln, 1)
            e.wait_ge(s_ln, 3)
            v.tensor_scalar(stat[:, 8:8 + T], stat[:, 8:8 + T], 1.0 / CONV, LN_EPS, ALU.mult, ALU.add).then_inc(s_ln, 1)
            e.wait_ge(s_lnp, 2)
            for t in range(T):
                i = v.tensor_scalar(ctok[:, t, :], ctok[:, t, :], stat[:, 8 + t:9 + t], None, ALU.mult)
            i.then_inc(s_ln, 1)
            for q in range(3):
                e.wait_ge(w.s.thi, w.at("t", 1))
                v.tensor_tensor(clo[:, 2 * q:2 * q + 2, :], hn[:, 0, 0:512].rearrange("p (a s) -> p a s", s=S),
                                chi[:, 2 * q:2 * q + 2, :].bitcast(F32), ALU.subtract).then_inc(w.s.tfree, 1)
                w.n["t"] += 1
            attention(w, [([None], None, 6 + i // 2 if i % 2 else None, None) for i in range(4)])
            for c in range(2):
                add_rows(w, chunk(w, 4, last), c, s_h)
            if stop < 2:
                return
            norm_rows(w, h, lambda k: sp("cvf", k, 1))
            for c in range(FF1 // 256):
                banks = chunk(w, 4, last)
                e.wait_ge(s_silu, c + 1)
                x = sg[:, c % 2, :]
                w.link(v.tensor_tensor(x, x, banks[1][:, :], ALU.mult))
                e.sem_inc(A.free)
                e.sem_inc(s_act)
                e.wait_ge(s_fhi, c + 1)
                v.tensor_tensor(flo[:, 2 * c:2 * c + 2, :], x.rearrange("p (a s) -> p a s", s=S),
                                fhi[:, 2 * c:2 * c + 2, :].bitcast(F32), ALU.subtract).then_inc(s_frdy, 1)
            for c in range(2):
                add_rows(w, chunk(w, FF1 // 256, last), c, s_h)
            if stop < 4:
                return
            norm_rows(w, h, lambda k: sp("swn", k, 1))
            for c in range(3):
                banks = chunk(w, 4, last)
                for t in range(T):
                    i = v.tensor_copy(z[:, t, c * 512:(c + 1) * 512], banks[t][:, :])
                w.link(i)
                e.sem_inc(A.free)
                e.sem_inc(s_ev)
            head_norm(w, [(scratch[:, 0:2048].rearrange("p (t n) -> p t n", t=T), z[:, :, 0:1024], 32, 16),
                          (scratch[:, 2048:2560].rearrange("p (t n) -> p t n", t=T), z[:, :, 1280:1536], 64, 4)], 20)
            turned_heads(w, [(qkT[:, 2 * i:2 * i + 2, :], 2, sp("swq")) for i in range(3)]
                         + [(qkT[:, 6:8, :], 2, sp("swk")), (qkT[:, 8:10, :], 2, sp("swmq"))])
            attention(w, [([mask["dist"]] if i < 12 else [None], sp("sinks", i, 1) if i < 12 else None,
                           i // 2 if i % 2 else None, co("slope", i, 1) if i < 12 else None) for i in range(16)])
            for c in range(2):
                add_rows(w, chunk(w, 4, last), c, s_h)
            if stop < 6:
                return
            for x in (outhi, outlo):
                for c in range(2):
                    i = v.tensor_scalar(x[:, c, :], co("dist"), 0.0, None, ALU.mult)
            i.then_inc(s_ol, 1)
            v.tensor_scalar(selT[:, :, :].rearrange("p t n -> p (t n)"), co("dist", 0, S), 0.0, None, ALU.mult
                            ).then_inc(s_ol, 1)
            v.memset(jobcur[:, 1, :], 0.0)
            norm_rows(w, h, lambda k: sp("swf", k, 1))
            e.wait_ge(s_tok, 1)
            v.tensor_tensor(toklo[:, :, :], hn[:, :, :], tokhi[:, :, :].bitcast(F32), ALU.subtract).then_inc(s_tokl, 1)
            R = scratch
            lg = R[:, 0:16].rearrange("p (t n) -> p t n", t=T)
            e.wait_ge(s_rt, 1)
            w.link(v.tensor_copy(R[:, 0:16], SC[0][:, 0:16]))
            top = R[:, 16:18]
            w.link(v.tensor_reduce(top, lg, axis=AX.X, op=ALU.max))
            gt = [R[:, 64 + 64 * t:128 + 64 * t].rearrange("p (a b) -> p a b", b=NE) for t in range(T)]
            eq = [R[:, 192 + 64 * t:256 + 64 * t].rearrange("p (a b) -> p a b", b=NE) for t in range(T)]
            low = co("low").rearrange("p (a b) -> p a b", b=NE)
            for t in range(T):
                other = lg[:, t, :].unsqueeze(1).to_broadcast([P, NE, NE])
                own = lg[:, t, :].unsqueeze(2).to_broadcast([P, NE, NE])
                w.link(v.tensor_tensor(gt[t], other, own, ALU.is_gt))
                w.link(v.tensor_tensor(eq[t], other, own, ALU.is_equal))
                w.link(v.tensor_tensor(eq[t], eq[t], low, ALU.mult))
                w.link(v.tensor_tensor(gt[t], gt[t], eq[t], ALU.add))
                w.link(v.reduce_sum(R[:, 24 + 8 * t:32 + 8 * t], gt[t], axis=AX.X))
            chosen = R[:, 40:56]
            v.tensor_scalar(chosen, R[:, 24:40], 1.5, None, ALU.is_lt).then_inc(s_rv, 1)
            for t in range(T):
                i = v.tensor_scalar(stat[:, 128 + 8 * t:136 + 8 * t], lg[:, t, :], top[:, t:t + 1], None, ALU.subtract)
            i.then_inc(s_rv, 1)
            e.wait_ge(s_rv, 1)
            e.wait_ge(s_ra, 1)
            gate = stat[:, 128:144]
            w.link(v.tensor_tensor(gate, gate, chosen, ALU.mult))
            w.link(v.reduce_sum(R[:, 18:20], gate.rearrange("p (t n) -> p t n", t=T), axis=AX.X))
            w.link(v.reciprocal(R[:, 18:20], R[:, 18:20]))
            for t in range(T):
                w.link(v.tensor_scalar(gate[:, 8 * t:8 * t + 8], gate[:, 8 * t:8 * t + 8], R[:, 18 + t:19 + t], None,
                                       ALU.mult))
            e.wait_ge(s_rt, 2)
            pos = R[:, 320:336]
            cnt = R[:, 336:344]
            w.link(v.tensor_scalar(pos, SC[1][:, 0:16], 1000.0, None, ALU.add))
            w.link(v.tensor_tensor(pos, pos, chosen, ALU.mult))
            w.link(v.tensor_scalar(pos, pos, -1000.0, None, ALU.add))
            w.link(v.tensor_copy(cnt, SC[1][:, 16:24]))
            nj, more, first, end = R[:, 344:352], R[:, 352:360], R[:, 360:368], R[:, 368:376]
            w.link(v.tensor_scalar(nj, cnt, 0.5, None, ALU.is_gt))
            w.link(v.tensor_scalar(more, cnt, P + 0.5, None, ALU.is_gt))
            w.link(v.tensor_tensor(nj, nj, more, ALU.add))
            before = R[:, 384:448].rearrange("p (a b) -> p a b", b=NE)
            w.link(v.tensor_tensor(before, nj.unsqueeze(1).to_broadcast([P, NE, NE]), low, ALU.mult))
            w.link(v.reduce_sum(first, before, axis=AX.X))
            w.link(v.tensor_tensor(end, first, nj, ALU.add))
            jobs_c = co("jobs").rearrange("p (a b) -> p a b", b=NE)
            exps_c = co("experts").rearrange("p (a b) -> p a b", b=NE)
            wide = [P, MAXJOB, NE]
            whose = R[:, 448:544].rearrange("p (a b) -> p a b", b=NE)
            tmp = R[:, 544:640].rearrange("p (a b) -> p a b", b=NE)
            off = R[:, 640:652]
            w.link(v.tensor_tensor(whose, jobs_c, first.unsqueeze(1).to_broadcast(wide), ALU.is_ge))
            w.link(v.tensor_tensor(tmp, jobs_c, end.unsqueeze(1).to_broadcast(wide), ALU.is_lt))
            w.link(v.tensor_tensor(whose, whose, tmp, ALU.mult))
            w.link(v.tensor_tensor(tmp, jobs_c, first.unsqueeze(1).to_broadcast(wide), ALU.subtract))
            w.link(v.tensor_tensor(tmp, tmp, whose, ALU.mult))
            w.link(v.reduce_sum(off, tmp, axis=AX.X))
            w.link(v.tensor_scalar(off, off, float(P), None, ALU.mult))
            for t in range(T):
                w.link(v.tensor_tensor(tmp, whose, pos[:, 8 * t:8 * t + 8].unsqueeze(1).to_broadcast(wide), ALU.mult))
                w.link(v.reduce_sum(jobpos[:, t, :], tmp, axis=AX.X))
                w.link(v.tensor_tensor(jobpos[:, t, :], jobpos[:, t, :], off, ALU.subtract))
                w.link(v.tensor_tensor(tmp, whose, gate[:, 8 * t:8 * t + 8].unsqueeze(1).to_broadcast(wide), ALU.mult))
                w.link(v.reduce_sum(jobgate[:, t, :], tmp, axis=AX.X))
            w.link(v.tensor_tensor(tmp, whose, exps_c, ALU.mult))
            w.link(v.reduce_sum(R[:, 661:661 + MAXJOB], tmp, axis=AX.X))
            w.link(v.reduce_sum(R[:, 660:661], nj, axis=AX.X))
            v.tensor_copy(tab[0:1, :], R[0:1, 660:661 + MAXJOB]).then_inc(s_tab, 1)
            e.wait_ge(s_tab, 1)
            jobs = e.value_load(tab[0:1, 0:1], min_val=1, max_val=MAXJOB - 1)

            def select(position):
                w.link(v.tensor_copy(jobcur[:, 0, :], position))
                for t in range(T):
                    i = v.tensor_scalar(sel[:, t, :], co("iota"), jobcur[:, 0, t:t + 1], None, ALU.is_equal)
                i.then_inc(s_sel, 1)

            def gathered_lo(n):
                e.wait_ge(s_xhi, n)
                for k in range(KD):
                    i = v.scalar_tensor_tensor(xlo[:, k, 0:P], SC[k // 4][:, (k % 4) * P:(k % 4 + 1) * P],
                                               sp("swf", k, 1), xhi[:, k, 0:P].bitcast(F32), ALU.mult, ALU.subtract)
                i.then_inc(s_xj, 1)

            def hidden_lo(c):
                e.wait_ge(w.s.thi, w.at("t", 1))
                v.tensor_tensor(mlo[:, 2 * c:2 * c + 2, :], TB[w.n["t"] % 2][:, 0:S].rearrange("p (a s) -> p a s", s=P),
                                mhi[:, 2 * c:2 * c + 2, :].bitcast(F32), ALU.subtract).then_inc(w.s.tfree, 1)
                w.n["t"] += 1

            def add_scattered(c, job):
                e.wait_ge(s_scat, job * 2 + (c + 1))
                for t in range(T):
                    x = h[:, t, c * 512:(c + 1) * 512]
                    i = v.scalar_tensor_tensor(x, SC[t][:, :], jobcur[:, 1, t:t + 1], x, ALU.mult, ALU.add)
                i.then_inc(s_h, 1)

            last = 1 << 30
            select(jobpos[:, :, 0])
            gathered_lo(1)
            split_to(w, w.n["p"] + LOOK)
            with e.Fori(0, jobs) as j:
                w.loop(j, PER_JOB)
                for c in range(FFE // 256):
                    banks = chunk(w, 4, last)
                    e.wait_ge(s_silu, j * 14 + (FF1 // 256 + c + 1))
                    x = sg[:, c % 2, 0:256]
                    v.tensor_tensor(hn[:, c % 2, 0:256], x, banks[0][:, 256:512], ALU.mult).then_inc(s_act, 1)
                    e.wait_ge(s_act, j * 14 + (FF1 // 256 + c + 1))
                    e.sem_inc(w.s.free)
                    if c >= 1:
                        hidden_lo(c - 1)
                    if c in (1, 2):
                        add_scattered(c - 1, j)
                    if c == 3:
                        e.wait_ge(s_h, j * 2 + 8)
                        w.link(v.tensor_copy(jobcur[:, 1, :], jobgate[:, :, bass.ds(j, 1)].rearrange("p t a -> p (t a)")))
                        for t in range(T):
                            e.wait_ge(w.s.thi, w.at("t", 1))
                            v.tensor_copy(selT[:, t, HD:P], TB[w.n["t"] % 2][:, HD:P]).then_inc(w.s.tfree, 1)
                            w.n["t"] += 1
                        select(jobpos[:, :, bass.ds(j + 1, 1)].rearrange("p t a -> p (t a)"))
                split_to(w, w.n["p"] + 6)
                hidden_lo(FFE // 256 - 1)
                for c in range(2):
                    if c == 1:
                        gathered_lo(j + 2)
                    banks = chunk(w, KE // 2, last)
                    e.wait_ge(s_oh, j * 2 + (c + 1))
                    v.tensor_tensor(outlo[:, c, :], banks[0][:, :], outhi[:, c, :].bitcast(F32), ALU.subtract
                                    ).then_inc(s_ol, 1)
                    e.wait_ge(s_ol, j * 2 + (c + 3))
                    e.sem_inc(w.s.free)
                w.end(("p", "g", "t", "vd"))
            w.after(jobs)
            w.split = w.begin["p"] + LOOK
            split_to(w, w.n["p"] + SLOTS)
            for c in range(2):
                add_scattered(c, jobs)
            if stop < 7:
                return

            e.drain().then_inc(B.lo, SLOTS)
            e.drain().then_inc(B.free, 2)
            e.drain().then_inc(B.tfree, 2)
            e.drain().then_inc(B.sfree, 2)
            e.drain().then_inc(B.ofree, 2)
            e.drain().then_inc(s_res, 4)
            w = Walk(e, B, B.vd)
            with e.Fori(0, 2) as l:
                w.loop(l, PER_LAYER)
                last = PANELS_B
                v.tensor_copy(n2[:, :], small[:, bass.ds(l * 24 + SM["norms2"][0], 24)]).then_inc(s_par, 1)
                e.wait_ge(s_par, l + 1)
                split_to(w, LOOK)
                norm_rows(w, mbuf, lambda k: n2[:, k:k + 1])
                banks = chunk(w, 4, last)
                for t in range(T):
                    w.link(v.tensor_copy(mkv[:, t, :], banks[t][:, :]))
                e.sem_inc(B.free)
                e.sem_inc(s_z2)
                turned_heads(w, [(mkT, 2, 1.0)])
                norm_rows(w, h, lambda k: n2[:, 8 + k:9 + k])
                for c in range(11):
                    if c < 5:
                        banks = chunk(w, 4, last)
                        for t in range(T):
                            i = v.tensor_copy(z[:, t, c * 512:(c + 1) * 512], banks[t][:, :])
                        w.link(i)
                        e.sem_inc(B.free)
                        if c == 4:
                            for base in (0, 1152):
                                for t in range(T):
                                    x = z[:, t, base:base + 768].rearrange("p (a k) -> p a k", k=HD)[:, :, 0:16]
                                    a = scratch[:, 0:192].rearrange("p (a k) -> p a k", k=16)
                                    b = scratch[:, 192:384].rearrange("p (a k) -> p a k", k=16)
                                    cs = co("cosx", 16 * t, 16).unsqueeze(1).to_broadcast([P, 12, 16])
                                    s1 = co("sinx", 16 * t, 8).unsqueeze(1).to_broadcast([P, 12, 8])
                                    s2 = co("sinx", 16 * t + 8, 8).unsqueeze(1).to_broadcast([P, 12, 8])
                                    w.mark(v.tensor_tensor(a, x, cs, ALU.mult))
                                    w.mark(v.tensor_tensor(b[:, :, 0:8], x[:, :, 8:16], s1, ALU.mult))
                                    w.link(v.tensor_tensor(b[:, :, 8:16], x[:, :, 0:8], s2, ALU.mult))
                                    w.link(v.tensor_tensor(x, a, b, ALU.add))
                            e.sem_inc(B.zrdy)
                    else:
                        w.n["p"] += 4
                        split_to(w, min(w.n["p"] + LOOK, last))
                        w.n["g"] += 1
                turned_heads(w, [(qkT[:, a[0]:a[-1] + 1, :], len(a), 0.125 if kind == "q" else 1.0)
                                 for a, kind in GROUPS2])
                attention(w, [([mask["win"], mask["dil4"], mask["dil16"]], None, 0 if i % 2 else None, None)
                              for i in range(2)]
                          + [([mask["causal"]], None, 1 + i // 2 if i % 2 else None, None) for i in range(6)]
                          + [([None], None, 4 + i // 2 if i % 2 else None, None) for i in range(4)])
                for n in range(2):
                    for br in range(3):
                        banks = chunk(w, [1, 2, 1][br], last)
                        for t in range(T):
                            gt_ = gates[:, t, br * D + n * 512:br * D + (n + 1) * 512]
                            y = hn[:, t, n * 512:(n + 1) * 512]
                            if br == 0:
                                i = v.tensor_tensor(y, gt_, banks[t][:, :], ALU.mult)
                            else:
                                w.link(v.tensor_tensor(gt_, gt_, banks[t][:, :], ALU.mult))
                                i = v.tensor_tensor(y, y, gt_, ALU.add)
                        w.link(i)
                        e.sem_inc(B.free)
                e.sem_inc(s_y2)
                turned(w, None)
                for c in range(2):
                    add_rows(w, chunk(w, 4, last), c, s_res)
                norm_rows(w, h, lambda k: n2[:, 16 + k:17 + k])
                for c in range(8):
                    banks = chunk(w, 4, last)
                    for b in range(2):
                        n = 2 * c + b
                        e.wait_ge(s_r2, l * 16 + n + 1)
                        if b == 1:
                            e.sem_inc(B.free)
                        x = sg[:, b, :]
                        v.tensor_tensor(x, x, x, ALU.mult).then_inc(s_q2, 1)
                    for b in range(2):
                        n = 2 * c + b
                        e.wait_ge(s_h2, l * 16 + n + 1)
                        k = 4 * c + 2 * b
                        v.tensor_tensor(flo[:, k:k + 2, :], sg[:, b, :].rearrange("p (a s) -> p a s", s=S),
                                        fhi[:, k:k + 2, :].bitcast(F32), ALU.subtract).then_inc(s_l2, 1)
                for c in range(2):
                    add_rows(w, chunk(w, 16, last), c, s_res)
                w.end(("p", "g", "t", "n", "s", "a", "r", "o", "vd"))
            w.it = None
            w.n["n"] = 6
            e.wait_ge(B.nss, 7)
            v.tensor_scalar(stat[:, 0:T], stat[:, 0:T], 1.0 / D, EPS, ALU.mult, ALU.add).then_inc(B.nms, 1)
            e.wait_ge(B.nr, 7)
            e.wait_ge(s_gf, 16)
            for t in range(T):
                i = v.scalar_tensor_tensor(hn[:, t, :], h[:, t, :], stat[:, t:t + 1], mbuf[:, 0, :], ALU.mult, ALU.mult)
            i.then_inc(B.nhn, 1)

        @block.tensor
        def _(e):
            mm, tr = nc.tensor.matmul, nc.tensor.transpose

            def chunk_tokens(w, lhi, llo, panels, ntok=T, width=512, k0=0, before=None):
                e.wait_ge(w.s.free, w.at("g", 1))
                g, k, n = w.n["g"], k0, sum(panels)
                for step, tiles in enumerate(panels):
                    if before is not None:
                        before(step)
                    e.wait_ge(w.s.lo, w.at("p", 1 + SLOTS))
                    slot = w.n["p"] % SLOTS
                    for kk in range(tiles):
                        cols = slice(kk * 512, kk * 512 + width)
                        for t in range(ntok):
                            row = slice(t * P, (t + 1) * P)
                            for q, (x, y) in enumerate(((lhi, whi), (lhi, wlo), (llo, whi))):
                                i = mm(L[2 * (g % 2) + t][:, 0:width], x[:, k, row], y[:, slot, cols],
                                       start=(k == k0 and q == 0), stop=(k == k0 + n - 1 and q == 2))
                        k += 1
                    i.then_inc(w.s.used, 1)
                    w.n["p"] += 1
                w.n["g"] += 1

            def chunk_features(w):
                e.wait_ge(w.s.free, w.at("g", 1))
                g = w.n["g"]
                for j in range(4):
                    e.wait_ge(w.s.lo, w.at("p", 1 + SLOTS))
                    slot = w.n["p"] % SLOTS
                    for kk in range(2):
                        k = 2 * j + kk
                        for f in range(4):
                            cols = slice(kk * 512 + f * P, kk * 512 + (f + 1) * P)
                            out = L[2 * (g % 2) + f // 2][:, (f % 2) * S:(f % 2 + 1) * S]
                            for q, (x, y) in enumerate(((whi, xhi), (wlo, xhi), (whi, xlo))):
                                i = mm(out, x[:, slot, cols], y[:, k, :], start=(k == 0 and q == 0 and f % 2 == 0),
                                       stop=(k == KD - 1 and q == 2 and f % 2 == 1), skip_group_check=True)
                    i.then_inc(w.s.used, 1)
                    w.n["p"] += 1
                w.n["g"] += 1

            def turn(w, tiles):
                e.wait_ge(w.s.tfree, w.at("t", 1))
                for c, src in tiles:
                    i = tr(TB[w.n["t"] % 2][:, c:c + P], src, ident)
                i.then_inc(w.s.tdone, 1)
                w.n["t"] += 1

            def turn_rows(w, src, ready):
                e.wait_ge(*ready)
                for q in range(4):
                    turn(w, [(kk * S + t * P, src[:, t, (2 * q + kk) * P:(2 * q + kk + 1) * P])
                             for kk in range(2) for t in range(T)])

            def norm(w):
                turn_rows(w, hn, (w.s.nhn, w.at("n", 1)))
                w.n["n"] += 1
                e.wait_ge(w.s.tfree, w.at("t", 2))

            def pair_src(src, cols, t):
                return src[:, t, cols:cols + P]

            def attention(w, heads):
                def scores(i):
                    for qp, row, key, _ in heads[i][0]:
                        e.wait_ge(w.s.sfree, w.at("s", 1))
                        for t in range(T):
                            ins = mm(SC[w.n["s"] % 2][:, t * S:(t + 1) * S], qkT[row:row + HD, qp, t * P:(t + 1) * P],
                                     key, start=True, stop=True)
                        ins.then_inc(w.s.sdone, 1)
                        w.n["s"] += 1

                plan = score_slots([len(x[0]) for x in heads])

                def transposes(i, j):
                    r = w.n["r"]
                    e.wait_ge(w.s.rcopy, w.at("r", 1))
                    for kt in range(2):
                        for t in range(T):
                            ins = tr(TB[r % 2][:, kt * S + t * P:kt * S + (t + 1) * P],
                                     SMX[:, plan[i][0] + j, t, kt * P:(kt + 1) * P], ident)
                    ins.then_inc(w.s.rdone, 1)
                    w.n["r"] += 1

                def values(i, j, later):
                    tiles, ends = heads[i]
                    if i % 2 == 0 and j == 0:
                        e.wait_ge(w.s.ofree, w.at("o", 1))
                    e.wait_ge(w.s.rcopy, w.at("r", 2 - later))
                    half, r = (i % 2) * HD, w.n["r"] - 1 - later
                    for kt in range(2):
                        ins = mm(L[w.n["o"] % 2][half:half + HD, 0:S], tiles[j][3](kt), PT[:, r % 2, kt * S:(kt + 1) * S],
                                 start=(j == 0 and kt == 0), stop=(j == len(tiles) - 1 and kt == 1))
                    ins.then_inc(w.s.pv, 1)
                    if ends and j == len(tiles) - 1:
                        w.n["o"] += 1

                e.wait_ge(w.s.tfree, w.at("t", 2))
                scores(0)
                scores(1)
                before = None
                for i in range(len(heads)):
                    if i + 2 < len(heads):
                        scores(i + 2)
                    e.wait_ge(w.s.pr, w.at("a", i + 1))
                    for j in range(len(heads[i][0])):
                        transposes(i, j)
                        if before is not None:
                            values(*before, 1)
                        before = (i, j)
                values(*before, 0)
                w.n["a"] += len(heads)
                e.wait_ge(w.s.ofree, w.at("o", 2))

            def mem_value(hh):
                return lambda kt: mkv[:, kt, 256 + hh * HD:256 + (hh + 1) * HD]

            def mem_heads(pair0):
                return [([(pair0 + hh // 2, (hh % 2) * HD, mkT[(hh % 2) * HD:(hh % 2 + 1) * HD, hh // 2, :],
                           mem_value(hh))], hh % 2 == 1) for hh in range(4)]

            for s in (A.used, ):
                e.drain().then_inc(s, SLOTS)
            e.drain().then_inc(A.rcopy, 2)
            e.drain().then_inc(A.pv, 2)
            w = Walk(e, A)
            e.wait_ge(s_in[0], 16)
            norm(w)
            chunk_tokens(w, xhi, xlo, FULL)
            e.wait_ge(A.zrdy, 1)
            turn(w, [(c * S + t * P, mkv[:, t, c * P:(c + 1) * P]) for c in range(2) for t in range(T)])
            norm(w)
            for c in range(3):
                chunk_features(w)
            chunk_tokens(w, xhi, xlo, FULL, width=256)
            e.wait_ge(A.zrdy, 2)
            turn(w, [(c * S + t * P, z[:, t, c * P:(c + 1) * P]) for c in range(2) for t in range(T)])
            for q in range(3):
                e.wait_ge(s_conv, q + 1)
                turn(w, [(t * S + kk * P, cacc[:, 2 * q + kk, t * P:(t + 1) * P]) for kk in range(2) for t in range(T)])
            e.wait_ge(s_ln, 5)
            for q in range(3):
                turn(w, [(kk * S + t * P, ctok[:, t, (2 * q + kk) * P:(2 * q + kk + 1) * P])
                         for kk in range(2) for t in range(T)])
            attention(w, mem_heads(0))
            for c in range(2):
                chunk_tokens(w, chi, clo, FULL)
            if stop < 2:
                return
            norm(w)
            for c in range(FF1 // 256):
                chunk_features(w)
            e.wait_ge(s_frdy, FF1 // 256)
            for c in range(2):
                chunk_tokens(w, fhi, flo, [2] * (FF1 // 256))
            if stop < 4:
                return
            norm(w)
            for c in range(3):
                chunk_tokens(w, xhi, xlo, FULL)
            e.wait_ge(A.zrdy, 3)

            for i in range(3):
                turn(w, [(c * S + t * P, z[:, t, (2 * i + c) * P:(2 * i + c + 1) * P]) for c in range(2) for t in range(T)])
            for base in (768, 1280):
                turn(w, [(c * S + t * P, z[:, t, base + c * P:base + (c + 1) * P]) for c in range(2) for t in range(T)])

            def window_head(i):
                kv = i // 3
                row = (kv % 2) * HD
                return ([((kv // 2) * 3 + i % 3, row, qkT[row:row + HD, 6 + kv // 2, :],
                          lambda kt: z[:, kt, 1024 + kv * HD:1024 + (kv + 1) * HD])], i % 2 == 1)
            attention(w, [window_head(i) for i in range(12)] + mem_heads(8))
            for c in range(2):
                chunk_tokens(w, chi, clo, FULL)
            if stop < 6:
                return
            norm(w)
            e.wait_ge(s_pre, 6)
            for t in range(T):
                for k in range(KD):
                    for q, (x, y) in enumerate(((xhi, rhi), (xhi, rlo), (xlo, rhi))):
                        i = mm(SC[0][:, t * NE:(t + 1) * NE], x[:, k, t * P:(t + 1) * P], y[:, k * NE:(k + 1) * NE],
                               start=(k == 0 and q == 0), stop=(k == KD - 1 and q == 2))
            i.then_inc(s_rt, 1)
            e.wait_ge(s_rv, 1)
            tri = co("tri")
            pick = [scratch[:, 40 + 8 * t:48 + 8 * t] for t in range(T)]
            mm(SC[1][:, 0:8], tri, pick[0], start=True, stop=True)
            mm(SC[1][:, 8:16], co("ones"), pick[0], start=True, stop=False)
            mm(SC[1][:, 8:16], tri, pick[1], start=False, stop=True)
            mm(SC[1][:, 16:24], co("ones"), pick[0], start=True, stop=False)
            mm(SC[1][:, 16:24], co("ones"), pick[1], start=False, stop=True).then_inc(s_rt, 1)
            e.wait_ge(s_tab, 1)
            jobs = e.value_load(tab[0:1, 0:1], min_val=1, max_val=MAXJOB - 1)

            def gather(n):
                e.wait_ge(s_sel, n)
                for k in range(KD):
                    out = SC[k // 4][:, (k % 4) * P:(k % 4 + 1) * P]
                    for t in range(T):
                        for q, x in enumerate((tokhi, toklo)):
                            i = mm(out, x[:, t, k * P:(k + 1) * P], sel[:, t, :], start=(t == 0 and q == 0),
                                   stop=(t == 1 and q == 1))
                i.then_inc(s_gat, 1)

            def scatter(c):
                for t in range(T):
                    for q, y in enumerate((outhi, outlo)):
                        i = mm(SC[t][:, :], selT[:, t, :], y[:, c, :], start=(q == 0), stop=(q == 1))
                i.then_inc(s_scat, 1)

            e.wait_ge(s_tokl, 1)
            gather(1)
            with e.Fori(0, jobs) as j:
                w.loop(j, PER_JOB)
                e.wait_ge(s_xj, j + 1)

                def turn_hidden(c):
                    e.wait_ge(s_act, j * 14 + (FF1 // 256 + c + 1))
                    turn(w, [(kk * P, hn[:, c % 2, kk * P:(kk + 1) * P]) for kk in range(2)])

                for c in range(FFE // 256):
                    chunk_tokens(w, xhi, xlo, FULL, ntok=1)
                    if c >= 1:
                        turn_hidden(c - 1)
                    if c == 1:
                        e.wait_ge(s_ol, j * 2 + 2)
                        scatter(0)
                    if c == 2:
                        e.wait_ge(s_h, j * 2 + 7)
                        scatter(1)
                    if c == 3:
                        for t in range(T):
                            turn(w, [(0, sel[:, t, :].bitcast(F32))])

                def hidden_ready(i):
                    if i == 0:
                        e.wait_ge(w.s.tfree, w.at("t", 1))
                    if i == 3:
                        turn_hidden(FFE // 256 - 1)
                    if i == 12:
                        e.wait_ge(w.s.tfree, w.at("t", 1))
                    if i == 13:
                        e.wait_ge(w.s.tfree, w.at("t", 2))

                chunk_tokens(w, mhi, mlo, [2] * (KE // 2), ntok=1, before=hidden_ready)
                e.wait_ge(s_h, j * 2 + 8)
                gather(j + 2)
                chunk_tokens(w, mhi, mlo, [2] * (KE // 2), ntok=1)
                w.end("pgt")
            e.wait_ge(s_ol, jobs * 2 + 2)
            e.wait_ge(s_xj, jobs + 1)
            scatter(0)
            e.wait_ge(s_h, jobs * 2 + 7)
            scatter(1)
            if stop < 7:
                return

            e.wait_ge(s_res, 4)
            e.drain().then_inc(B.used, SLOTS)
            e.drain().then_inc(B.rcopy, 2)
            e.drain().then_inc(B.pv, 2)
            w = Walk(e, B)
            with e.Fori(0, 2) as l:
                w.loop(l, PER_LAYER)
                norm(w)
                chunk_tokens(w, xhi, xlo, FULL)
                e.wait_ge(s_z2, l + 1)
                turn(w, [(c * S + t * P, mkv[:, t, c * P:(c + 1) * P]) for c in range(2) for t in range(T)])
                norm(w)
                for c in range(11):
                    chunk_tokens(w, xhi, xlo, FULL)
                e.wait_ge(B.zrdy, l + 1)
                for pairs, _ in GROUPS2:
                    turn(w, [(c * S + t * P, z[:, t, PAIRS2[a]:PAIRS2[a] + P]) for c, a in enumerate(pairs)
                             for t in range(T)])
                e.wait_ge(B.tfree, w.at("t", 2))

                def head2(x, q0, k0, vcol):
                    row = (x % 2) * HD
                    return (q0 + x // 2, row, qkT[row:row + HD, k0 + x // 2, :],
                            lambda kt: z[:, kt, vcol + x * HD:vcol + (x + 1) * HD])
                attention(w, [([head2(2 * g + i, 0, 3, 768) for g in range(3)], i == 1) for i in range(2)]
                          + [([head2(x, 6, 9, 1920)], x % 2 == 1) for x in range(6)] + mem_heads(12))
                for n in range(2):
                    chunk_tokens(w, chi, clo, [1], k0=0)
                    chunk_tokens(w, chi, clo, [2, 1], k0=1)
                    chunk_tokens(w, chi, clo, [2], k0=4)
                turn_rows(w, hn, (s_y2, l + 1))
                e.wait_ge(w.s.tfree, w.at("t", 2))
                for c in range(2):
                    chunk_tokens(w, xhi, xlo, FULL)
                norm(w)
                for c in range(8):
                    chunk_features(w)
                e.wait_ge(s_l2, l * 16 + 16)
                for c in range(2):
                    chunk_tokens(w, fhi, flo, [2] * 16)
                w.end("pgtnsaro")


def chunks_of(w, width=512):
    k, n = w.shape
    kp, nc_ = -(-k // 256), -(-n // 512)
    out = np.zeros((nc_, kp, P, 2, 512), w.dtype)
    for c in range(nc_):
        cols = w[:, c * 512:(c + 1) * 512]
        for i in range(k // P):
            out[c, i // 2, :, i % 2, 0:cols.shape[1]] = cols[i * P:(i + 1) * P]
    return out.reshape(nc_ * kp, P, 1024)


def paired(a, b):
    k, n = a.shape
    both = np.stack([x.reshape(k // 256, 2, P, n // 256, 256).transpose(3, 0, 2, 1, 4) for x in (a, b)], axis=4)
    return both.reshape(n // 256 * (k // 256), P, 1024)


def tiles(v):
    return v.reshape(-1, P).T


def constants():
    i = np.arange(P)
    tok = np.arange(S)
    dist = (tok[:, None] - tok[None, :]).astype(np.float32)
    rows = lambda m: m.reshape(T, P, S).transpose(1, 0, 2).reshape(P, T * S)
    blocked = lambda ok: rows(np.where(ok, np.float32(0), np.float32(-1e30)))
    causal = dist >= 0
    e8 = np.arange(NE)
    inv = (1.0 / (np.float32(500000.0) ** (np.arange(0, 16, 2, dtype=np.float32) / np.float32(16)))).astype(np.float32)
    ang = tok.astype(np.float32)[:, None] * inv[None, :]
    cos, sin = np.cos(ang).astype(np.float32), np.sin(ang).astype(np.float32)
    per = lambda m: m.reshape(T, P, 16).transpose(1, 0, 2).reshape(P, T * 16)
    wide = lambda v: np.broadcast_to(v.reshape(1, -1), (P, v.size))
    c = dict(
        ident=np.eye(P), tri=(i[:, None] < i[None, :]), ones=np.ones((P, P)), iota=wide(i),
        slope=wide(-np.exp2(-8.0 * (np.arange(12) + 1.0) / 12)),
        low=wide((e8[None, :] < e8[:, None]).astype(np.float32)),
        jobs=wide(np.repeat(np.arange(MAXJOB), NE)), experts=wide(np.tile(e8, MAXJOB)),
        dist=rows(np.where(causal & (dist < 128), dist, np.float32(1e33))),
        win=blocked(causal & (dist <= 128)), dil4=blocked(causal & (dist % 4 == 0)),
        dil16=blocked(causal & (dist % 16 == 0)), causal=blocked(causal),
        cosx=per(np.concatenate([cos, cos], 1)), sinx=per(np.concatenate([-sin, sin], 1)))
    return np.ascontiguousarray(np.concatenate([np.asarray(c[k], np.float32).reshape(P, n) for k, n in CONST.items()], 1))


def kernel(**a):
    import concourse.bacc as bacc
    from concourse.bass_utils import run_bass_kernel_spmd as run
    a = {k: np.asarray(v) for k, v in a.items()}
    two = lambda g: np.concatenate([g, g]).reshape(P, 1)
    cv, sw = a["cv_w_in"][0], a["sw_w_in"][0]
    order = [x + 3 * y + 6 * g for g in range(2) for x in range(3) for y in range(2)]
    sw = np.concatenate([sw[:, i * HD:(i + 1) * HD] for i in order] + [sw[:, 768:]], 1)
    w1 = np.concatenate([
        chunks_of(a["w_mem_kv"]), paired(cv[:, 0:CONV], cv[:, CONV:2 * CONV]), chunks_of(cv[:, 2 * CONV:]),
        chunks_of(a["cv_w_out"][0]), paired(a["cv_w_gate"][0], a["cv_w_up"][0]), chunks_of(a["cv_w_down"][0]),
        chunks_of(sw), chunks_of(a["sw_w_out"][0])])
    wm = np.concatenate([x for e in range(NE) for x in (
        paired(a["sw_we_gate"][0, e], a["sw_we_up"][0, e]), chunks_of(a["sw_we_down"][0, e]))])
    w2 = []
    for l in range(2):
        pa, pb, pm = (chunks_of(a[f"w_proj_{b}_2"][l]) for b in "abm")
        w2 += [chunks_of(a["w_mem_kv_2"][l]), chunks_of(a["w_in_2"][l])]
        for n in range(2):
            w2 += [pa[n:n + 1], pb[2 * n:2 * n + 2], pm[n:n + 1]]
        w2 += [chunks_of(a["w_out_2"][l]), chunks_of(a["w_up_2"][l]), chunks_of(a["w_down_2"][l])]
    w2 = np.concatenate(w2)
    parts = dict(
        mem_g=tiles(a["mem_norm_g"]), cvn=tiles(a["cv_attn_norm_g"][0]), cvf=tiles(a["cv_ffn_norm_g"][0]),
        swn=tiles(a["sw_attn_norm_g"][0]), swf=tiles(a["sw_ffn_norm_g"][0]), bglu=tiles(a["cv_b_glu"][0]),
        dww=a["cv_dw_w"][0].reshape(TAPS, FC, P).transpose(2, 1, 0).reshape(P, FC * TAPS),
        dwb=tiles(a["cv_dw_b"][0]), lng=tiles(a["cv_ln_g"][0]), lnb=tiles(a["cv_ln_b"][0]),
        memk=two(a["mem_k_norm_g"]), cvq=two(a["cv_memq_norm_g"][0]), swmq=two(a["sw_memq_norm_g"][0]),
        swq=two(a["sw_q_norm_g"][0]), swk=two(a["sw_k_norm_g"][0]),
        sinks=np.broadcast_to(a["sw_sinks"][0].reshape(1, 12), (P, 12)),
        router=a["sw_router"][0].reshape(KD, P, NE).transpose(1, 0, 2).reshape(P, KD * NE),
        norms2=np.concatenate([tiles(a[k][l]) for l in range(2) for k in ("norm_mem_2", "norm_mix_2", "norm_mlp_2")], 1))
    small = np.concatenate([parts[k] for k in SMALL], 1)
    arrays = dict(x=a["x"][0], mem=a["mem"][0], mem2=a["mem_2"][0], w1=w1, wm=wm, w2=w2, small=small,
                  const=constants(), gfin=np.broadcast_to(a["norm_final_2"].reshape(1, D), (P, D)))
    arrays = {k: np.ascontiguousarray(v) for k, v in arrays.items()}
    nc = bacc.Bacc("TRN2", target_bir_lowering=False, num_devices=1)
    d = {k: nc.dram_tensor(k, v.shape, mybir.dt.from_np(v.dtype), kind="ExternalInput").ap() for k, v in arrays.items()}
    d["out"] = nc.dram_tensor("out", (S, D), F32, kind="ExternalOutput").ap()
    build(nc, d, STOP)
    r = run(nc, [arrays], core_ids=[0])
    return r.results[0]["out"].reshape(1, S, D)


STOP = 99
```

```python
import numpy as np
import concourse.bass as bass
from concourse import mybir
from contextlib import ExitStack

F32, F32R, I32 = mybir.dt.float32, mybir.dt.float32r, mybir.dt.int32
ACT, ALU, AX = mybir.ActivationFunctionType, mybir.AluOpType, mybir.AxisListType

P = 128
T = 2
S = T * P
D = 1024
KD = D // P
HD = 64
EPS, LN_EPS = 1e-6, 1e-5
CONV, TAPS = 768, 31
FC = CONV // P
PAD = TAPS - 1
TAPS_PE = 12
TAPS_V = TAPS - TAPS_PE
FF1 = 2816
NE, FFE = 8, 3584
KE = FFE // P
FF2 = 4096
MAXJOB = 12
SLOTS = 4
DEEP = 7
LOOK = 3
QKV2 = 2560
TILES_SMX = 6

FULL = [2, 2, 2, 2]
PANELS_A = 4 + 3 * 4 + 4 + 8 + (FF1 // 256) * 4 + 2 * (FF1 // 256) + 12 + 8
PANELS_M = (FFE // 256) * 4 + 2 * (KE // 2)
PANELS_B = 4 + 11 * 4 + 8 + 8 + 8 * 4 + 2 * 16

PER_JOB = dict(p=PANELS_M, g=16, t=16, n=0, h=0, s=0, a=0, r=0, o=0, va=0, vd=2)
PER_LAYER = dict(p=PANELS_B, g=30, t=26, n=2, h=0, s=16, a=12, r=16, o=6, va=0, vd=53)

SMALL = dict(mem_g=8, cvn=8, cvf=8, swn=8, swf=8, bglu=12, dww=FC * TAPS, dwb=FC, lng=FC, lnb=FC,
             memk=1, cvq=1, swmq=1, swq=1, swk=1, sinks=12, router=KD * NE, norms2=48)
CONST = dict(ident=P, tri=P, ones=P, iota=P, slope=12, low=64, jobs=MAXJOB * NE, experts=MAXJOB * NE,
             dist=2 * S, win=2 * S, dil4=2 * S, dil16=2 * S, causal=2 * S, cosx=T * 16, sinx=T * 16)


def columns(table):
    at, out = 0, {}
    for name, n in table.items():
        out[name] = (at, n)
        at += n
    return out, at


SM, NSM = columns(SMALL)
CO, NCO = columns(CONST)
MASKS = CO["dist"][0]

PAIRS2 = [128 * i for i in range(3)] + [384 + 128 * i for i in range(3)] \
    + [1152 + 128 * i for i in range(3)] + [1536 + 128 * i for i in range(3)] + [2304, 2432]
GROUPS2 = [([0, 1], 'q'), ([2], 'q'), ([3, 4], 'k'), ([5], 'k'), ([6, 7], 'q'), ([8], 'q'),
           ([9, 10], 'k'), ([11], 'k'), ([12, 13], 'q')]


def score_slots(counts):
    plan, owner, at = [], [None] * TILES_SMX, 0
    for i, n in enumerate(counts):
        at = at if at + n <= TILES_SMX else 0
        users = [owner[at + j] for j in range(n) if owner[at + j] is not None]
        plan.append((at, max(users) if users else None, sum(counts[:i])))
        owner[at:at + n] = [i] * n
        at = (at + n) % TILES_SMX
    return plan


def head_stats(stat, i):
    c = 80 + 6 * (i % 4)
    return stat[:, c:c + 2], stat[:, c + 2:c + 4], stat[:, c + 4:c + 6]


def build(nc, d):
    ctx = ExitStack()
    with ctx:
        cursor = [16512]

        def sb(name, shape, dt, at=None):
            size = int(np.prod(shape[1:])) * 4
            if at is None:
                at = cursor[0]
                cursor[0] += (size + 31) // 32 * 32
            return nc.alloc_sbuf_tensor_at(name, shape, dt, offset=at)

        raw = sb("raw", [P, SLOTS, 1024], F32)
        qkT = sb("qkT", [P, 14, S], F32)
        deep = sb("deep", [P, DEEP, 1024], F32, 16512)
        assert DEEP * 4096 <= SLOTS * 4096 + 14 * S * 4
        whi = sb("whi", [P, SLOTS, 1024], F32R)
        wlo = sb("wlo", [P, SLOTS, 1024], F32R)
        h = sb("h", [P, T, D], F32)
        xhi = sb("xhi", [P, KD, S], F32R)
        xlo = sb("xlo", [P, KD, S], F32R)
        region = cursor[0]
        cursor[0] += 65536
        fhi = sb("fhi", [P, FF2 // P, S], F32R, region)
        flo = sb("flo", [P, FF2 // P, S], F32R, region + 32768)
        mhi = sb("mhi", [P, KE, P], F32R, region)
        mlo = sb("mlo", [P, KE, P], F32R, region + 14336)
        tokhi = sb("tokhi", [P, T, D], F32R, region + 28672)
        toklo = sb("toklo", [P, T, D], F32R, region + 36864)
        outhi = sb("outhi", [P, T, 512], F32R, region + 45056)
        outlo = sb("outlo", [P, T, 512], F32R, region + 49152)
        z = sb("z", [P, T, QKV2], F32, region)
        gates = sb("gates", [P, T, 3 * D], F32, region + 20480)
        chi = sb("chi", [P, KD, S], F32R, region + 45056)
        clo = sb("clo", [P, KD, S], F32R, region + 53248)
        u = sb("u", [P, FC, PAD + S], F32, region + 20480)
        cacc = sb("cacc", [P, FC, S], F32, region + 20480 + 6912)
        ctok = sb("ctok", [P, T, CONV], F32, region + 20480 + 13056)

        hn = sb("hn", [P, T, D], F32)
        mbuf = sb("mbuf", [P, T, D], F32)
        mkv = sb("mkv", [P, T, 512], F32)
        mkT = sb("mkT", [P, 2, S], F32)
        SMX = sb("SMX", [P, TILES_SMX, T, S], F32)
        scratch = SMX[:, :, :, :].rearrange("p a c d -> p (a c d)")
        PT = sb("PT", [P, 2, 2 * S], F32)
        sg = sb("sg", [P, 2, 512], F32)
        smx_at = cursor[0] - (TILES_SMX * T * S + 2 * 2 * S + 2 * 512) * 4
        diag = [sb(f"diag{k}", [P, TAPS_PE, P], F32, at) for k, at in enumerate(
            (region + 45056, region + 51200, smx_at, smx_at + 6144, region + 1024, region + 11264))]
        small = sb("small", [P, NSM], F32)
        const = sb("const", [P, NCO], F32)
        stat = sb("stat", [P, 160], F32)
        halfneg = sb("halfneg", [P, 1], F32)
        n2 = sb("n2", [P, 24], F32)
        jobpos = sb("jobpos", [P, T, MAXJOB], F32, region + 61952)
        jobgate = sb("jobgate", [P, T, MAXJOB], F32, region + 62048)
        jobcur = sb("jobcur", [P, 2, T], F32)
        sel = sb("sel", [P, T, P], F32R, region + 53248)
        selT = sb("selT", [P, T, P], F32R, region + 54272)
        rhi = sb("rhi", [P, KD * NE], F32R, region + 61440)
        rlo = sb("rlo", [P, KD * NE], F32R, region + 61696)
        tab = sb("tab", [1, 1 + MAXJOB], I32)
        assert cursor[0] <= 229344, cursor[0]

        def sp(name, a=0, n=None):
            c, m = SM[name]
            return small[:, c + a:c + a + (m if n is None else n)]

        def co(name, a=0, n=None):
            c, m = CO[name]
            return const[:, c + a:c + a + (m if n is None else n)]

        ident = co("ident")
        mask = {k: co(k) for k in ("dist", "win", "dil4", "dil16", "causal")}

        L = [ctx.enter_context(nc.psum_tensor(f"L{i}", [P, 512], F32)) for i in range(4)]
        SC = [ctx.enter_context(nc.psum_tensor(f"SC{i}", [P, 512], F32)) for i in range(2)]
        TB = [ctx.enter_context(nc.psum_tensor(f"TB{i}", [P, 512], F32)) for i in range(2)]

        def sem(name):
            return ctx.enter_context(nc.semaphore(name))

        class Signals:
            def __init__(self, q):
                self.raw = [sem(f"{q}raw{i}") for i in range(SLOTS)]
                self.ring = (raw, self.raw, 0)
                self.hi = sem(q + "hi")
                self.lo = sem(q + "lo")
                self.used = sem(q + "used")
                self.free = sem(q + "free")
                self.tdone = sem(q + "tdone")
                self.thi = sem(q + "thi")
                self.tfree = sem(q + "tfree")
                self.nss = sem(q + "nss")
                self.nms = sem(q + "nms")
                self.nr = sem(q + "nr")
                self.nhn = sem(q + "nhn")
                self.hsq = sem(q + "hsq")
                self.hms = sem(q + "hms")
                self.hr = sem(q + "hr")
                self.zrdy = sem(q + "zrdy")
                self.sdone = sem(q + "sdone")
                self.sfree = sem(q + "sfree")
                self.mx = sem(q + "mx")
                self.ex = sem(q + "ex")
                self.pr = sem(q + "pr")
                self.rdone = sem(q + "rdone")
                self.rcopy = sem(q + "rcopy")
                self.pv = sem(q + "pv")
                self.ohi = sem(q + "ohi")
                self.ofree = sem(q + "ofree")
                self.va = sem(q + "va")
                self.vd = sem(q + "vd")

        A, B = Signals("a_"), Signals("b_")
        s_deep = [sem(f"s_deep{i}") for i in range(DEEP)]
        s_gf = sem("s_gf")
        s_in = [sem(f"s_in{i}") for i in range(4)]
        s_masks = sem("s_masks")
        s_mem2 = sem("s_mem2")
        s_out = sem("s_out")
        s_pre = sem("s_pre")
        s_ev = sem("s_ev")
        s_sig = sem("s_sig")
        s_diag = sem("s_diag")
        s_tap = sem("s_tap")
        s_conv = sem("s_conv")
        s_ln = sem("s_ln")
        s_lnp = sem("s_lnp")
        s_silu = sem("s_silu")
        s_act = sem("s_act")
        s_fhi = sem("s_fhi")
        s_frdy = sem("s_frdy")
        s_h = sem("s_h")
        s_tok = sem("s_tok")
        s_tokl = sem("s_tokl")
        s_rt = sem("s_rt")
        s_rv = sem("s_rv")
        s_ra = sem("s_ra")
        s_tab = sem("s_tab")
        s_sel = sem("s_sel")
        s_gat = sem("s_gat")
        s_xhi = sem("s_xhi")
        s_xj = sem("s_xj")
        s_scat = sem("s_scat")
        s_oh = sem("s_oh")
        s_ol = sem("s_ol")
        s_r2 = sem("s_r2")
        s_q2 = sem("s_q2")
        s_h2 = sem("s_h2")
        s_l2 = sem("s_l2")
        s_z2 = sem("s_z2")
        s_y2 = sem("s_y2")
        s_res = sem("s_res")
        s_par = sem("s_par")

        class Walk:
            def __init__(self, e, s, chain=None):
                self.e, self.s, self.chain = e, s, chain
                self.key = "va" if chain is s.va else "vd"
                self.n = dict.fromkeys(PER_JOB, 0)
                self.split = 0
                self.ring = s.ring
                self.it, self.per = None, None

            def at(self, kind, plus=0):
                v = self.n[kind] + plus
                return v if self.it is None else self.it * self.per[kind] + v

            def loop(self, it, per):
                self.it, self.per, self.begin = it, per, dict(self.n)

            def after(self, turns):
                self.it, self.n = turns, dict(self.begin)

            def end(self, kinds):
                for k in kinds:
                    got = self.n[k] - self.begin[k]
                    assert got == self.per[k], (k, got, self.per[k])

            def mark(self, ins):
                self.n[self.key] += 1
                ins.then_inc(self.chain, 1)
                return self.at(self.key)

            def need(self, value):
                self.e.wait_ge(self.chain, value)

            def link(self, ins):
                self.need(self.mark(ins))

        def output_bank(w):
            return L[2 * ((w.n["g"] + 1) % 2) + w.n["o"] % 2]

        def window_block(c):
            cols = ((0, 512), (512, 1024), (1280, 1536))[c]
            n = T * (cols[1] - cols[0])
            return cols, scratch[:, 1024 * c:1024 * c + n].rearrange("p (t n) -> p t n", t=T)

        block = ctx.enter_context(nc.Block())

        @block.sync
        def _(e):
            def panels(s, source, n, first=0, it=None, per=0):
                for i in range(n):
                    p = first + i
                    v = p + 1 if it is None else it * per + (p + 1)
                    e.wait_ge(s.lo, v)
                    e.dma_start(raw[:, p % SLOTS, :], source(i)).then_inc(s.raw[p % SLOTS], 16)

            e.dma_start(mbuf[:, :, :], d["mem"].rearrange("(t p) n -> p t n", p=P)).then_inc(s_in[3], 16)
            e.wait_ge(s_in[3], 16)
            first = 8
            panels(A, lambda i: d["w1"][i], first)
            e.wait_ge(A.nhn, 1)
            e.dma_start(mbuf[:, :, :], d["mem2"].rearrange("(t p) n -> p t n", p=P)).then_inc(s_mem2, 16)
            rest = PANELS_A - first
            turns = rest // SLOTS
            with e.Fori(0, turns) as k:
                for i in range(SLOTS):
                    p = first + i
                    e.wait_ge(A.lo, k * SLOTS + (p + 1))
                    e.dma_start(raw[:, p % SLOTS, :], d["w1"][bass.ds(k * SLOTS + p, 1)].rearrange("a p n -> p (a n)")
                                ).then_inc(A.raw[p % SLOTS], 16)
            done = first + turns * SLOTS
            panels(A, lambda i: d["w1"][done + i], PANELS_A - done, done)
            hout = d["out"].rearrange("(t p) n -> p t n", p=P)
            e.wait_ge(s_tab, 1)
            jobs = e.value_load(tab[0:1, 0:1], min_val=1, max_val=MAXJOB - 1)

            def expert_panel(expert, panel, slot, split):
                e.wait_ge(A.lo, split)
                e.dma_start(deep[:, slot, :], d["wm"][bass.ds(expert * PANELS_M + panel, 1)].rearrange("a p n -> p (a n)")
                            ).then_inc(s_deep[slot], 16)

            expert = e.value_load(tab[0:1, 1:2], min_val=0, max_val=NE - 1)
            for i in range(DEEP):
                expert_panel(expert, i, i, PANELS_A + SLOTS)
            split = PANELS_A + SLOTS + 1
            with e.Fori(0, jobs) as j:
                expert = e.value_load(tab[0:1, bass.ds(j + 1, 1)], min_val=0, max_val=NE - 1)
                with e.Fori(0, PANELS_M // DEEP - 1) as k:
                    for i in range(DEEP):
                        expert_panel(expert, k * DEEP + (DEEP + i), i, j * PANELS_M + k * DEEP + (split + i))
                follower = e.value_load(tab[0:1, bass.ds(j + 2, 1)], min_val=0, max_val=NE - 1)
                for i in range(DEEP):
                    expert_panel(follower, i, i, j * PANELS_M + (PANELS_M - DEEP + split + i))
            for i in range(DEEP):
                e.wait_ge(s_deep[i], jobs * (16 * PANELS_M // DEEP) + 16)
            panels(B, lambda i: d["w2"][i], SLOTS)
            with e.Fori(0, 2 * PANELS_B // SLOTS - 1) as k:
                for i in range(SLOTS):
                    e.wait_ge(B.lo, k * SLOTS + (SLOTS + i + 1))
                    e.dma_start(raw[:, i, :], d["w2"][bass.ds(k * SLOTS + (SLOTS + i), 1)].rearrange("a p n -> p (a n)")
                                ).then_inc(B.raw[i], 16)
            e.wait_ge(B.nhn, 4)
            e.dma_start(mbuf[:, 0, :], d["gfin"]).then_inc(s_gf, 16)
            e.wait_ge(B.nhn, 5)
            e.dma_start(hout, hn[:, :, :]).then_inc(s_out, 16)
            e.wait_ge(s_out, 16)

        @block.gpsimd
        def _(e):
            e.memset(halfneg[:, :], -0.5).then_inc(s_lnp, 1)
            e.wait_ge(s_lnp, 1)

            def power(ready, v, src, n, done):
                e.wait_ge(ready, v)
                e.tensor_tensor(src, src, halfneg[:, 0:1].to_broadcast([P, n]), ALU.pow).then_inc(done, 1)

            def row(w):
                power(w.s.nms, w.at("n", 1), stat[:, 0:T], T, w.s.nr)
                w.n["n"] += 1

            def heads(w, nh, at=32):
                power(w.s.hms, w.at("h", 1), stat[:, at:at + T * nh], T * nh, w.s.hr)
                w.n["h"] += 1

            w = Walk(e, A)
            row(w)
            heads(w, 4)
            row(w)
            heads(w, 4)
            power(s_ln, 4, stat[:, 8:8 + T], T, s_lnp)
            row(w)
            row(w)
            row(w)
            heads(w, 8)
            heads(w, 8, 48)
            heads(w, 4, 64)
            row(w)
            w = Walk(e, B)
            with e.Fori(0, 2) as l:
                w.loop(l, PER_LAYER)
                for _ in range(2):
                    row(w)
                w.end("n")
            w.it, w.n["n"] = None, 4
            row(w)

        @block.scalar
        def _(e):
            act = nc.scalar.activation

            def split_to(w, target):
                while w.split < target:
                    p = w.split
                    w.split += 1
                    slots, loaded, first = w.ring
                    depth = len(loaded)
                    slot, base = (p - first) % depth, 16 * ((p - first) // depth + 1)
                    e.wait_ge(loaded[slot], base if w.it is None else w.it * (16 * w.per["p"] // depth) + base)
                    q = p + 1
                    e.wait_ge(w.s.used, q if w.it is None else w.it * w.per["p"] + q)
                    act(whi[:, p % SLOTS, :], slots[:, slot, :], ACT.Copy).then_inc(w.s.hi, 1)

            def chunk(w, np_, last):
                w.n["p"] += np_
                split_to(w, min(w.n["p"] + LOOK, last))
                w.n["g"] += 1


            def complete(w):
                e.wait_ge(w.s.used, w.at("p", SLOTS))

            def norm(w, src, ready, gain):
                squares(w, src, ready)
                turned(w, gain)

            def squares(w, src, ready):
                e.wait_ge(*ready)
                e.wait_ge(w.s.tfree, w.at("t", 2))
                for t in range(T):
                    i = act(hn[:, t, :], src[:, t, :], ACT.Square, accum_out=stat[:, t:t + 1])
                i.then_inc(w.s.nss, 1)
                w.n["n"] += 1

            def turned(w, gain, out=None):
                e.wait_ge(w.s.used, w.at("p", SLOTS))
                for q in range(4):
                    e.wait_ge(w.s.tdone, w.at("t", 1))
                    bank = TB[w.n["t"] % 2]
                    for kk in range(2):
                        k = 2 * q + kk
                        i = act((xhi if out is None else out)[:, k, :], bank[:, kk * S:(kk + 1) * S], ACT.Copy,
                                scale=1.0 if gain is None else gain(k))
                    i.then_inc(w.s.thi, 1)
                    w.n["t"] += 1

            def head_squares(w, parts):
                e.wait_ge(*parts[0])
                for src, dst in parts[1]:
                    i = act(dst, src, ACT.Square)
                i.then_inc(w.s.hsq, 1)
                w.n["h"] += 1

            def turned_heads(w, groups):
                for dst, n, scale in groups:
                    e.wait_ge(w.s.tdone, w.at("t", 1))
                    bank = TB[w.n["t"] % 2][:, 0:n * S].rearrange("p (a s) -> p a s", s=S)
                    act(dst[:, :, 0:P], bank[:, :, 0:P], ACT.Copy, scale=scale).then_inc(w.s.thi, 1)
                    w.n["t"] += 1

            def attention(w, heads):
                plan = score_slots([len(x[0]) for x in heads])

                def exps(i):
                    parts, sink, _ = heads[i]
                    slot, n = plan[i][0], len(parts)
                    neg_max, total, sunk = head_stats(stat, i)
                    e.wait_ge(w.s.mx, w.at("a", i + 1))
                    for t in range(T):
                        x = SMX[:, slot:slot + n, t, :]
                        ins = act(x, x, ACT.Exp, bias=neg_max[:, t:t + 1], accum_out=total[:, t:t + 1])
                    if sink is not None:
                        ins = act(sunk, neg_max, ACT.Exp, bias=sink)
                    ins.then_inc(w.s.ex, 1)

                def copies(i):
                    for _ in heads[i][0]:
                        e.wait_ge(w.s.rdone, w.at("r", 1))
                        e.wait_ge(w.s.pv, w.at("r", 1))
                        r = w.n["r"]
                        act(PT[:, r % 2, :], TB[r % 2][:, :], ACT.Copy).then_inc(w.s.rcopy, 1)
                        w.n["r"] += 1

                r0 = w.n["r"]

                def pair_out(i):
                    done = r0 - w.n["r"] + plan[i][2] + len(heads[i][0])
                    e.wait_ge(w.s.pv, w.at("r", done + 2))
                    act(chi[:, heads[i][2], :], output_bank(w)[:, 0:S], ACT.Copy).then_inc(w.s.ohi, 1)
                    w.n["o"] += 1

                exps(0)
                exps(1)
                for i in range(len(heads)):
                    copies(i)
                    if i + 2 < len(heads):
                        exps(i + 2)
                    if i >= 1 and heads[i - 1][2] is not None:
                        pair_out(i - 1)
                pair_out(len(heads) - 1)
                w.n["a"] += len(heads)

            e.dma_start(small[:, :], d["small"]).then_inc(s_in[1], 16)
            e.dma_start(const[:, 0:MASKS], d["const"][:, 0:MASKS]).then_inc(s_in[0], 16)
            e.wait_ge(s_in[3], 16)
            e.dma_start(const[:, MASKS:NCO], d["const"][:, MASKS:NCO]).then_inc(s_masks, 16)
            e.dma_start(h[:, :, :], d["x"].rearrange("(t p) n -> p t n", p=P)).then_inc(s_in[2], 16)

            w = Walk(e, A, A.va)
            last = PANELS_A
            e.wait_ge(s_in[1], 16)
            squares(w, mbuf, (s_in[3], 16))
            split_to(w, LOOK)
            turned(w, lambda k: sp("mem_g", k, 1))

            def diagonal_chunk(c):
                w.n["p"] += 4
                for step in range(4):
                    split_to(w, w.n["p"] + LOOK - 3 + step)
                    for i in range(step * TAPS_PE // 4, (step + 1) * TAPS_PE // 4):
                        for k in (2 * c, 2 * c + 1):
                            ins = act(diag[k][:, i, :], ident, ACT.Copy, scale=sp("dww", k * TAPS + TAPS_V + i, 1))
                ins.then_inc(s_diag, 1)
                w.n["g"] += 1

            chunk(w, 4, last)
            head_squares(w, ((s_ev, 1), [(mkv[:, :, 0:256], scratch[:, 0:512].rearrange("p (t n) -> p t n", t=T))]))
            turned_heads(w, [(mkT, 2, sp("memk"))])
            norm(w, h, (s_in[2], 16), lambda k: sp("cvn", k, 1))
            for c in range(3):
                diagonal_chunk(c)
                complete(w)
                g = w.n["g"] - 1
                e.wait_ge(s_ev, 1 + c)
                for f in range(2):
                    i = act(sg[:, 0, f * S:(f + 1) * S], L[2 * (g % 2) + 1][:, f * S:(f + 1) * S], ACT.Sigmoid,
                            bias=sp("bglu", FC + 2 * c + f, 1))
                i.then_inc(s_sig, 1)
            chunk(w, 4, last)
            head_squares(w, ((s_ev, 5), [(z[:, :, 0:256], scratch[:, 0:512].rearrange("p (t n) -> p t n", t=T))]))
            turned_heads(w, [(qkT[:, 0:2, :], 2, sp("cvq"))])
            for q in range(3):
                e.wait_ge(w.s.tdone, w.at("t", 1))
                act(ctok[:, 0, q * S:(q + 1) * S], TB[w.n["t"] % 2][:, 0:S], ACT.Copy).then_inc(w.s.thi, 1)
                w.n["t"] += 1
            e.wait_ge(w.s.tfree, w.at("t", 2))
            for t in range(T):
                i = act(hn[:, t, 0:CONV], ctok[:, t, :], ACT.Copy, accum_out=stat[:, 8 + t:9 + t])
            i.then_inc(s_ln, 1)
            e.wait_ge(s_ln, 2)
            for t in range(T):
                i = act(hn[:, t, 0:CONV], ctok[:, t, :], ACT.Square, accum_out=stat[:, 8 + t:9 + t])
            i.then_inc(s_ln, 1)
            for q in range(3):
                e.wait_ge(w.s.tdone, w.at("t", 1))
                for kk in range(2):
                    k = 2 * q + kk
                    m = w.mark(act(hn[:, 0, kk * S:(kk + 1) * S], TB[w.n["t"] % 2][:, kk * S:(kk + 1) * S], ACT.Silu,
                                   scale=sp("lng", k, 1), bias=sp("lnb", k, 1)))
                w.need(m)
                act(chi[:, 2 * q:2 * q + 2, :], hn[:, 0, 0:512].rearrange("p (a s) -> p a s", s=S), ACT.Copy
                    ).then_inc(w.s.thi, 1)
                w.n["t"] += 1
                e.wait_ge(w.s.tfree, w.at("t", 2))
            attention(w, [([0], None, None), ([0], None, 6), ([0], None, None), ([0], None, 7)])
            for c in range(2):
                chunk(w, 4, last)
            norm(w, h, (s_h, 2), lambda k: sp("cvf", k, 1))

            for c in range(FF1 // 256):
                chunk(w, 4, last)
                complete(w)
                g = w.n["g"] - 1
                if c >= 2:
                    e.wait_ge(s_frdy, c - 1)
                act(sg[:, c % 2, :], L[2 * (g % 2)][:, :], ACT.Silu).then_inc(s_silu, 1)
                e.wait_ge(s_act, c + 1)
                act(fhi[:, 2 * c:2 * c + 2, :], sg[:, c % 2, :].rearrange("p (a s) -> p a s", s=S), ACT.Copy
                    ).then_inc(s_fhi, 1)
            squares(w, mbuf, (s_mem2, 16))
            for c in range(2):
                chunk(w, FF1 // 256, last)
            norm(w, h, (s_h, 4), lambda k: sp("swn", k, 1))
            for c in range(3):
                chunk(w, 4, last)
                cols, sq = window_block(c)
                head_squares(w, ((s_ev, 6 + c), [(z[:, :, cols[0]:cols[1]], sq)]))
            turned_heads(w, [(qkT[:, 2 * i:2 * i + 2, :], 2, sp("swq")) for i in range(3)]
                         + [(qkT[:, 6:8, :], 2, sp("swk")), (qkT[:, 8:10, :], 2, sp("swmq"))])
            attention(w, [([0], sp("sinks", i, 1) if i < 12 else None, i // 2 if i % 2 else None) for i in range(16)])
            for c in range(2):
                chunk(w, 4, last)
            norm(w, h, (s_h, 6), lambda k: sp("swf", k, 1))
            act(tokhi[:, :, :], hn[:, :, :], ACT.Copy).then_inc(s_tok, 1)
            e.wait_ge(s_rv, 2)
            act(stat[:, 128:144], stat[:, 128:144], ACT.Exp).then_inc(s_ra, 1)
            e.wait_ge(s_tab, 1)
            jobs = e.value_load(tab[0:1, 0:1], min_val=1, max_val=MAXJOB - 1)

            def gathered_hi(n):
                e.wait_ge(s_gat, n)
                for k in range(KD):
                    i = act(xhi[:, k, 0:P], SC[k // 4][:, (k % 4) * P:(k % 4 + 1) * P], ACT.Copy, scale=sp("swf", k, 1))
                i.then_inc(s_xhi, 1)

            def hidden_hi(c):
                e.wait_ge(w.s.tdone, w.at("t", 1))
                act(mhi[:, 2 * c:2 * c + 2, :], TB[w.n["t"] % 2][:, 0:S].rearrange("p (a s) -> p a s", s=P),
                    ACT.Copy).then_inc(w.s.thi, 1)
                w.n["t"] += 1

            last = 1 << 30
            gathered_hi(1)
            w.ring = (deep, s_deep, PANELS_A)
            split_to(w, w.n["p"] + LOOK)
            with e.Fori(0, jobs) as j:
                w.loop(j, PER_JOB)
                for c in range(FFE // 256):
                    chunk(w, 4, last)
                    complete(w)
                    g = w.n["g"] - 1
                    e.wait_ge(s_act, j * 14 + (FF1 // 256 + max(c - 1, 0)))
                    act(sg[:, c % 2, 0:256], L[2 * (g % 2)][:, 0:256], ACT.Silu).then_inc(s_silu, 1)
                    if c >= 1:
                        hidden_hi(c - 1)
                    if c == 3:
                        for t in range(T):
                            e.wait_ge(w.s.tdone, w.at("t", 1))
                            act(selT[:, t, 0:HD], TB[w.n["t"] % 2][:, 0:HD], ACT.Copy).then_inc(w.s.thi, 1)
                            w.n["t"] += 1
                split_to(w, w.n["p"] + 6)
                hidden_hi(FFE // 256 - 1)
                for c in range(2):
                    if c == 1:
                        gathered_hi(j + 2)
                    chunk(w, KE // 2, last)
                    complete(w)
                    g = w.n["g"] - 1
                    act(outhi[:, c, :], L[2 * (g % 2)][:, :], ACT.Copy).then_inc(s_oh, 1)
                w.end("pgt")
            w.after(jobs)

            w = Walk(e, B, B.va)
            with e.Fori(0, 2) as l:
                w.loop(l, PER_LAYER)
                last = PANELS_B
                split_to(w, LOOK)
                e.wait_ge(s_par, l + 1)
                turned(w, lambda k: n2[:, k:k + 1], chi)
                e.wait_ge(s_h, jobs * 2 + 8)
                squares(w, h, (s_res, l * 4 + 0 + 4))
                chunk(w, 4, last)
                turned(w, lambda k: n2[:, 8 + k:9 + k])
                for c in range(11):
                    chunk(w, 4, last)
                    if c == 0:
                        turned_heads(w, [(mkT, 2, 1.0)])
                    if c >= 5:
                        complete(w)
                        g = w.n["g"] - 1
                        e.wait_ge(w.s.free, w.at("g", 1))
                        for t in range(T):
                            i = act(gates[:, t, (c - 5) * 512:(c - 4) * 512], L[2 * (g % 2) + t][:, :], ACT.Sigmoid)
                        i.then_inc(w.s.free, 1)
                turned_heads(w, [(qkT[:, a[0]:a[-1] + 1, :], len(a), 0.125 if kind == "q" else 1.0)
                                 for a, kind in GROUPS2])
                attention(w, [([0, 1, 2], None, None), ([0, 1, 2], None, 0)]
                          + [([0], None, 1 + i // 2 if i % 2 else None) for i in range(10)])
                for c in range(6):
                    chunk(w, [1, 2, 1][c % 3], last)
                turned(w, None)
                for c in range(2):
                    chunk(w, 4, last)
                norm(w, h, (s_res, l * 4 + 2 + 4), lambda k: n2[:, 16 + k:17 + k])
                for c in range(8):
                    chunk(w, 4, last)
                    complete(w)
                    g = w.n["g"] - 1
                    for b in range(2):
                        n = 2 * c + b
                        if n >= 2:
                            e.wait_ge(s_l2, l * 16 + n - 1)
                        act(sg[:, b, :], L[2 * (g % 2) + b][:, :], ACT.Relu).then_inc(s_r2, 1)
                    for b in range(2):
                        n = 2 * c + b
                        e.wait_ge(s_q2, l * 16 + n + 1)
                        act(fhi[:, 4 * c + 2 * b:4 * c + 2 * b + 2, :],
                            sg[:, b, :].rearrange("p (a s) -> p a s", s=S), ACT.Copy).then_inc(s_h2, 1)
                for c in range(2):
                    chunk(w, 16, last)
                w.end("pgtnaro")
            w.it = None
            e.wait_ge(s_res, 12)
            for t in range(T):
                i = act(hn[:, t, :], h[:, t, :], ACT.Square, accum_out=stat[:, t:t + 1])
            i.then_inc(B.nss, 1)

        @block.vector
        def _(e):
            v = nc.vector

            def split_to(w, target):
                while w.split < target:
                    p = w.split
                    w.split += 1
                    q = p + 1
                    slots, loaded, first = w.ring
                    e.wait_ge(w.s.hi, q if w.it is None else w.it * w.per["p"] + q)
                    v.tensor_tensor(wlo[:, p % SLOTS, :], slots[:, (p - first) % len(loaded), :], whi[:, p % SLOTS, :].bitcast(F32),
                                    ALU.subtract).then_inc(w.s.lo, 1)

            def chunk(w, np_, last):
                w.n["p"] += np_
                split_to(w, min(w.n["p"] + LOOK, last))
                e.wait_ge(w.s.used, w.at("p", SLOTS))
                e.wait_ge(w.s.free, w.at("g", 2))
                w.n["g"] += 1
                return L[2 * ((w.n["g"] - 1) % 2)], L[2 * ((w.n["g"] - 1) % 2) + 1]

            def norm(w):
                e.wait_ge(w.s.nss, w.at("n", 1))
                v.tensor_scalar(stat[:, 0:T], stat[:, 0:T], 1.0 / D, EPS, ALU.mult, ALU.add).then_inc(w.s.nms, 1)
                e.wait_ge(w.s.nr, w.at("n", 1))

            def scaled_rows(w, dst, src):
                norm(w)
                for t in range(T):
                    i = v.tensor_scalar(dst[:, t, :], src[:, t, :], stat[:, t:t + 1], None, ALU.mult)
                i.then_inc(w.s.nhn, 1)
                w.n["n"] += 1

            def norm_rows(w, src, gain):
                scaled_rows(w, hn, src)
                turned(w, gain)

            def turned(w, gain, out=None):
                hi, lo = (xhi, xlo) if out is None else out
                for q in range(4):
                    e.wait_ge(w.s.thi, w.at("t", 1))
                    bank = TB[w.n["t"] % 2]
                    for kk in range(2):
                        k = 2 * q + kk
                        i = v.scalar_tensor_tensor(lo[:, k, :], bank[:, kk * S:(kk + 1) * S],
                                                   1.0 if gain is None else gain(k), hi[:, k, :].bitcast(F32),
                                                   ALU.mult, ALU.subtract)
                    i.then_inc(w.s.tfree, 1)
                    w.n["t"] += 1

            def head_norm(w, sq, rows, c, n):
                head_sums(w, sq, c, n)
                head_scale(w, rows, c, n, w.n["h"] - 1)

            def head_sums(w, sq, c, n):
                e.wait_ge(w.s.hsq, w.at("h", 1))
                for t in range(T):
                    m = w.mark(v.reduce_sum(stat[:, c + t * n:c + (t + 1) * n],
                                            sq[:, t, :].rearrange("p (a k) -> p a k", k=HD), axis=AX.X))
                w.need(m)
                v.tensor_scalar(stat[:, c:c + T * n], stat[:, c:c + T * n], 1.0 / HD, EPS, ALU.mult, ALU.add
                                ).then_inc(w.s.hms, 1)
                w.n["h"] += 1

            def head_scale(w, rows, c, n, norm_index):
                e.wait_ge(w.s.hr, norm_index + 1)
                for t in range(T):
                    x = rows[:, t, :].rearrange("p (a k) -> p a k", k=HD)
                    r = stat[:, c + t * n:c + (t + 1) * n].unsqueeze(2).to_broadcast([P, n, HD])
                    i = v.tensor_tensor(x, x, r, ALU.mult)
                i.then_inc(w.s.zrdy, 1)

            def turned_heads(w, groups):
                for dst, n, scale in groups:
                    e.wait_ge(w.s.thi, w.at("t", 1))
                    bank = TB[w.n["t"] % 2][:, 0:n * S].rearrange("p (a s) -> p a s", s=S)
                    v.tensor_scalar(dst[:, :, P:S], bank[:, :, P:S], scale, None, ALU.mult).then_inc(w.s.tfree, 1)
                    w.n["t"] += 1

            def attention(w, heads):
                plan = score_slots([len(x[0]) for x in heads])

                def scores(i):
                    masks, sink, _, slope = heads[i]
                    slot, user, _ = plan[i]
                    if user is not None:
                        e.wait_ge(w.s.rdone, w.at("r", plan[user][2] + len(heads[user][0])))
                    for j, m in enumerate(masks):
                        e.wait_ge(w.s.sdone, w.at("s", 1))
                        src, dst = SC[w.n["s"] % 2][:, :], SMX[:, slot + j].rearrange("p t s -> p (t s)")
                        if slope is not None:
                            ins = v.scalar_tensor_tensor(dst, m, slope, src, ALU.mult, ALU.add)
                        elif m is not None:
                            ins = v.tensor_tensor(dst, src, m, ALU.add)
                        else:
                            ins = v.tensor_copy(dst, src)
                        ins.then_inc(w.s.sfree, 1)
                        w.n["s"] += 1
                    e.wait_ge(w.s.sfree, w.at("s", 2))
                    x = SMX[:, slot:slot + len(masks)].rearrange("p r t s -> p t r s")
                    mx = head_stats(stat, i)[0]
                    if sink is None:
                        v.tensor_reduce(mx, x, axis=AX.XY, op=ALU.max, negate=True).then_inc(w.s.mx, 1)
                    else:
                        w.link(v.tensor_reduce(mx, x, axis=AX.XY, op=ALU.max))
                        v.tensor_scalar(mx, mx, sink, -1.0, ALU.max, ALU.mult).then_inc(w.s.mx, 1)

                def probs(i):
                    masks, sink, _, _ = heads[i]
                    slot = plan[i][0]
                    _, den, sunk = head_stats(stat, i)
                    e.wait_ge(w.s.ex, w.at("a", i + 1))
                    if sink is not None:
                        w.link(v.tensor_tensor(den, den, sunk, ALU.add))
                    w.link(v.reciprocal(den, den))
                    for t in range(T):
                        x = SMX[:, slot:slot + len(masks), t, :]
                        ins = v.tensor_scalar(x, x, den[:, t:t + 1], None, ALU.mult)
                    ins.then_inc(w.s.pr, 1)

                def pair_out(tile):
                    e.wait_ge(w.s.ohi, w.at("o", 1))
                    v.tensor_tensor(clo[:, tile, :], output_bank(w)[:, 0:S], chi[:, tile, :].bitcast(F32), ALU.subtract
                                    ).then_inc(w.s.ofree, 1)
                    w.n["o"] += 1

                scores(0)
                scores(1)
                for i in range(len(heads)):
                    probs(i)
                    if i + 2 < len(heads):
                        scores(i + 2)
                    if i >= 2 and heads[i - 2][2] is not None:
                        pair_out(heads[i - 2][2])
                pair_out(heads[-1][2])
                w.n["r"] += sum(len(x[0]) for x in heads)
                w.n["a"] += len(heads)

            def add_rows(w, banks, n, done):
                for t in range(T):
                    x = h[:, t, n * 512:(n + 1) * 512]
                    i = v.tensor_tensor(x, banks[t][:, :], x, ALU.add)
                w.need(w.mark(i))
                e.sem_inc(w.s.free)
                e.sem_inc(done)

            w = Walk(e, A, A.vd)
            e.drain().then_inc(A.lo, SLOTS)
            e.drain().then_inc(A.free, 2)
            e.drain().then_inc(A.tfree, 2)
            e.drain().then_inc(A.sfree, 2)
            e.drain().then_inc(A.ofree, 2)
            v.memset(u[:, :, 0:PAD], 0.0).then_inc(s_pre, 1)
            e.wait_ge(s_in[0], 16)
            e.wait_ge(s_in[1], 16)
            for name in ("cvq", "swq", "swmq"):
                v.tensor_scalar(sp(name), sp(name), HD ** -0.5, None, ALU.mult).then_inc(s_pre, 1)
            v.tensor_copy(rhi[:, :], sp("router")).then_inc(s_pre, 1)
            e.wait_ge(s_pre, 5)
            v.tensor_tensor(rlo[:, :], sp("router"), rhi[:, :].bitcast(F32), ALU.subtract).then_inc(s_pre, 1)
            last = PANELS_A
            scaled_rows(w, hn, mbuf)
            split_to(w, LOOK)
            turned(w, lambda k: sp("mem_g", k, 1))
            banks = chunk(w, 4, last)
            for t in range(T):
                w.link(v.tensor_copy(mkv[:, t, :], banks[t][:, :]))
            e.sem_inc(A.free)
            e.sem_inc(s_ev)
            head_norm(w, scratch[:, 0:512].rearrange("p (t n) -> p t n", t=T), mkv[:, :, 0:256], 32, 4)
            turned_heads(w, [(mkT, 2, sp("memk"))])
            norm_rows(w, h, lambda k: sp("cvn", k, 1))
            marks = [None, None]

            def taps(c, begin, end):
                for tap in range(begin, end):
                    for f in range(2):
                        k = 2 * c + f
                        tapw = sp("dww", k * TAPS + tap, 1)
                        if tap == 0:
                            ins = v.tensor_scalar(cacc[:, k, :], u[:, k, 0:S], tapw, sp("dwb", k, 1), ALU.mult, ALU.add)
                        else:
                            w.need(marks[f])
                            ins = v.scalar_tensor_tensor(cacc[:, k, :], u[:, k, tap:tap + S], tapw, cacc[:, k, :],
                                                         ALU.mult, ALU.add)
                        marks[f] = w.mark(ins)

            def tapped_chunk(c):
                w.n["p"] += 4
                for i in range(4):
                    split_to(w, w.n["p"] + LOOK - 3 + i)
                    if c >= 1:
                        taps(c - 1, i * TAPS_V // 4, (i + 1) * TAPS_V // 4)
                if c >= 2:
                    add_taps(c - 2)
                w.n["p"] -= 4
                return chunk(w, 4, last)

            def add_taps(c):
                e.wait_ge(s_tap, c + 1)
                v.tensor_tensor(cacc[:, 2 * c:2 * c + 2, :], SC[c % 2][:, :].rearrange("p (a s) -> p a s", s=S),
                                cacc[:, 2 * c:2 * c + 2, :], ALU.add).then_inc(s_conv, 1)

            for c in range(3):
                banks = tapped_chunk(c)
                e.wait_ge(s_sig, c + 1)
                for f in range(2):
                    i = v.scalar_tensor_tensor(u[:, 2 * c + f, PAD:PAD + S], banks[0][:, f * S:(f + 1) * S],
                                               sp("bglu", 2 * c + f, 1), sg[:, 0, f * S:(f + 1) * S], ALU.add, ALU.mult)
                w.link(i)
                e.sem_inc(A.free)
                e.sem_inc(s_ev)
            banks = tapped_chunk(3)
            for t in range(T):
                w.link(v.tensor_copy(z[:, t, 0:256], banks[t][:, 0:256]))
            e.sem_inc(A.free)
            e.sem_inc(s_ev)
            head_norm(w, scratch[:, 0:512].rearrange("p (t n) -> p t n", t=T), z[:, :, 0:256], 32, 4)
            turned_heads(w, [(qkT[:, 0:2, :], 2, sp("cvq"))])
            add_taps(2)
            for q in range(3):
                e.wait_ge(w.s.thi, w.at("t", 1))
                v.tensor_copy(ctok[:, 1, q * S:(q + 1) * S], TB[w.n["t"] % 2][:, S:2 * S]).then_inc(w.s.tfree, 1)
                w.n["t"] += 1
            e.wait_ge(s_ln, 1)
            w.link(v.tensor_scalar(stat[:, 8:8 + T], stat[:, 8:8 + T], 1.0 / CONV, None, ALU.mult))
            for t in range(T):
                i = v.tensor_scalar(ctok[:, t, :], ctok[:, t, :], stat[:, 8 + t:9 + t], None, ALU.subtract)
            i.then_inc(s_ln, 1)
            e.wait_ge(s_ln, 3)
            v.tensor_scalar(stat[:, 8:8 + T], stat[:, 8:8 + T], 1.0 / CONV, LN_EPS, ALU.mult, ALU.add).then_inc(s_ln, 1)
            e.wait_ge(s_lnp, 2)
            for t in range(T):
                i = v.tensor_scalar(ctok[:, t, :], ctok[:, t, :], stat[:, 8 + t:9 + t], None, ALU.mult)
            i.then_inc(s_ln, 1)
            for q in range(3):
                e.wait_ge(w.s.thi, w.at("t", 1))
                v.tensor_tensor(clo[:, 2 * q:2 * q + 2, :], hn[:, 0, 0:512].rearrange("p (a s) -> p a s", s=S),
                                chi[:, 2 * q:2 * q + 2, :].bitcast(F32), ALU.subtract).then_inc(w.s.tfree, 1)
                w.n["t"] += 1
            attention(w, [([None], None, 6 + i // 2 if i % 2 else None, None) for i in range(4)])
            for c in range(2):
                add_rows(w, chunk(w, 4, last), c, s_h)
            norm_rows(w, h, lambda k: sp("cvf", k, 1))
            for c in range(FF1 // 256):
                banks = chunk(w, 4, last)
                e.wait_ge(s_silu, c + 1)
                x = sg[:, c % 2, :]
                w.link(v.tensor_tensor(x, x, banks[1][:, :], ALU.mult))
                e.sem_inc(A.free)
                e.sem_inc(s_act)
                e.wait_ge(s_fhi, c + 1)
                v.tensor_tensor(flo[:, 2 * c:2 * c + 2, :], x.rearrange("p (a s) -> p a s", s=S),
                                fhi[:, 2 * c:2 * c + 2, :].bitcast(F32), ALU.subtract).then_inc(s_frdy, 1)
            scaled_rows(w, mbuf, mbuf)
            for c in range(2):
                add_rows(w, chunk(w, FF1 // 256, last), c, s_h)
            norm_rows(w, h, lambda k: sp("swn", k, 1))

            def scale(c):
                cols, _ = window_block(c)
                head_scale(w, z[:, :, cols[0]:cols[1]], 32 + 16 * c, (8, 8, 4)[c], 2 + c)

            for c in range(3):
                banks = chunk(w, 4, last)
                for t in range(T):
                    i = v.tensor_copy(z[:, t, c * 512:(c + 1) * 512], banks[t][:, :])
                w.link(i)
                e.sem_inc(A.free)
                e.sem_inc(s_ev)
                if c >= 1:
                    scale(c - 1)
                head_sums(w, window_block(c)[1], 32 + 16 * c, (8, 8, 4)[c])
            scale(2)
            turned_heads(w, [(qkT[:, 2 * i:2 * i + 2, :], 2, sp("swq")) for i in range(3)]
                         + [(qkT[:, 6:8, :], 2, sp("swk")), (qkT[:, 8:10, :], 2, sp("swmq"))])
            e.wait_ge(s_masks, 16)
            attention(w, [([mask["dist"]] if i < 12 else [None], sp("sinks", i, 1) if i < 12 else None,
                           i // 2 if i % 2 else None, co("slope", i, 1) if i < 12 else None) for i in range(16)])
            for c in range(2):
                add_rows(w, chunk(w, 4, last), c, s_h)
            for x in (outhi, outlo):
                for c in range(2):
                    i = v.tensor_scalar(x[:, c, :], co("dist"), 0.0, None, ALU.mult)
            i.then_inc(s_ol, 1)
            v.tensor_scalar(selT[:, :, :].rearrange("p t n -> p (t n)"), co("dist", 0, S), 0.0, None, ALU.mult
                            ).then_inc(s_ol, 1)
            v.memset(jobcur[:, 1, :], 0.0)
            norm_rows(w, h, lambda k: sp("swf", k, 1))
            e.wait_ge(s_tok, 1)
            v.tensor_tensor(toklo[:, :, :], hn[:, :, :], tokhi[:, :, :].bitcast(F32), ALU.subtract).then_inc(s_tokl, 1)
            R = scratch
            lg = R[:, 0:16].rearrange("p (t n) -> p t n", t=T)
            e.wait_ge(s_rt, 1)
            w.link(v.tensor_copy(R[:, 0:16], SC[0][:, 0:16]))
            top = R[:, 16:18]
            w.link(v.tensor_reduce(top, lg, axis=AX.X, op=ALU.max))
            pairs = [P, T, NE, NE]
            gt, eq = (R[:, c:c + 128].rearrange("p (t a b) -> p t a b", t=T, b=NE) for c in (64, 192))
            low = co("low").rearrange("p (a b) -> p a b", b=NE)
            other, own = lg.unsqueeze(2).to_broadcast(pairs), lg.unsqueeze(3).to_broadcast(pairs)
            w.link(v.tensor_tensor(gt, other, own, ALU.is_gt))
            w.link(v.tensor_tensor(eq, other, own, ALU.is_equal))
            w.link(v.tensor_tensor(eq, eq, low.unsqueeze(1).to_broadcast(pairs), ALU.mult))
            w.link(v.tensor_tensor(gt, gt, eq, ALU.add))
            w.link(v.reduce_sum(R[:, 24:40].rearrange("p (t n) -> p t n", t=T), gt, axis=AX.X))
            chosen = R[:, 40:56]
            v.tensor_scalar(chosen, R[:, 24:40], 1.5, None, ALU.is_lt).then_inc(s_rv, 1)
            gate = stat[:, 128:144]
            gates_t = gate.rearrange("p (t n) -> p t n", t=T)
            v.tensor_tensor(gates_t, lg, top.unsqueeze(2).to_broadcast([P, T, NE]), ALU.subtract).then_inc(s_rv, 1)
            e.wait_ge(s_rv, 1)
            e.wait_ge(s_ra, 1)
            w.link(v.tensor_tensor(gate, gate, chosen, ALU.mult))
            w.link(v.reduce_sum(R[:, 18:20], gate.rearrange("p (t n) -> p t n", t=T), axis=AX.X))
            w.link(v.reciprocal(R[:, 18:20], R[:, 18:20]))
            w.link(v.tensor_tensor(gates_t, gates_t, R[:, 18:20].unsqueeze(2).to_broadcast([P, T, NE]), ALU.mult))
            e.wait_ge(s_rt, 2)
            pos = R[:, 320:336]
            cnt = R[:, 336:344]
            w.link(v.tensor_scalar(pos, SC[1][:, 0:16], 1000.0, None, ALU.add))
            w.link(v.tensor_tensor(pos, pos, chosen, ALU.mult))
            w.link(v.tensor_scalar(pos, pos, -1000.0, None, ALU.add))
            w.link(v.tensor_copy(cnt, SC[1][:, 16:24]))
            nj, more, first, end = R[:, 344:352], R[:, 352:360], R[:, 360:368], R[:, 368:376]
            w.link(v.tensor_scalar(nj, cnt, 0.5, None, ALU.is_gt))
            w.link(v.tensor_scalar(more, cnt, P + 0.5, None, ALU.is_gt))
            w.link(v.tensor_tensor(nj, nj, more, ALU.add))
            before = R[:, 384:448].rearrange("p (a b) -> p a b", b=NE)
            w.link(v.tensor_tensor(before, nj.unsqueeze(1).to_broadcast([P, NE, NE]), low, ALU.mult))
            w.link(v.reduce_sum(first, before, axis=AX.X))
            w.link(v.tensor_tensor(end, first, nj, ALU.add))
            jobs_c = co("jobs").rearrange("p (a b) -> p a b", b=NE)
            exps_c = co("experts").rearrange("p (a b) -> p a b", b=NE)
            wide = [P, MAXJOB, NE]
            whose = R[:, 448:544].rearrange("p (a b) -> p a b", b=NE)
            tmp = R[:, 544:640].rearrange("p (a b) -> p a b", b=NE)
            off = R[:, 640:652]
            w.link(v.tensor_tensor(whose, jobs_c, first.unsqueeze(1).to_broadcast(wide), ALU.is_ge))
            w.link(v.tensor_tensor(tmp, jobs_c, end.unsqueeze(1).to_broadcast(wide), ALU.is_lt))
            w.link(v.tensor_tensor(whose, whose, tmp, ALU.mult))
            w.link(v.tensor_tensor(tmp, jobs_c, first.unsqueeze(1).to_broadcast(wide), ALU.subtract))
            w.link(v.tensor_tensor(tmp, tmp, whose, ALU.mult))
            w.link(v.reduce_sum(off, tmp, axis=AX.X))
            w.link(v.tensor_scalar(off, off, float(P), None, ALU.mult))
            all_jobs = [P, T, MAXJOB, NE]
            both = R[:, 768:960].rearrange("p (t a b) -> p t a b", t=T, b=NE)
            whose_t = whose.unsqueeze(1).to_broadcast(all_jobs)
            pos_t = pos.rearrange("p (t n) -> p t n", t=T)
            w.link(v.tensor_tensor(both, whose_t, pos_t.unsqueeze(2).to_broadcast(all_jobs), ALU.mult))
            w.link(v.reduce_sum(jobpos[:, :, :], both, axis=AX.X))
            w.link(v.tensor_tensor(jobpos[:, :, :], jobpos[:, :, :], off.unsqueeze(1).to_broadcast([P, T, MAXJOB]),
                                   ALU.subtract))
            w.link(v.tensor_tensor(both, whose_t, gates_t.unsqueeze(2).to_broadcast(all_jobs), ALU.mult))
            w.link(v.reduce_sum(jobgate[:, :, :], both, axis=AX.X))
            w.link(v.tensor_tensor(tmp, whose, exps_c, ALU.mult))
            w.link(v.reduce_sum(R[:, 661:661 + MAXJOB], tmp, axis=AX.X))
            w.link(v.reduce_sum(R[:, 660:661], nj, axis=AX.X))
            v.tensor_copy(tab[0:1, :], R[0:1, 660:661 + MAXJOB]).then_inc(s_tab, 1)
            e.wait_ge(s_tab, 1)
            jobs = e.value_load(tab[0:1, 0:1], min_val=1, max_val=MAXJOB - 1)

            def select(position):
                w.link(v.tensor_copy(jobcur[:, 0, :], position))
                for t in range(T):
                    i = v.tensor_scalar(sel[:, t, :], co("iota"), jobcur[:, 0, t:t + 1], None, ALU.is_equal)
                i.then_inc(s_sel, 1)

            def gathered_lo(n):
                e.wait_ge(s_xhi, n)
                for k in range(KD):
                    i = v.scalar_tensor_tensor(xlo[:, k, 0:P], SC[k // 4][:, (k % 4) * P:(k % 4 + 1) * P],
                                               sp("swf", k, 1), xhi[:, k, 0:P].bitcast(F32), ALU.mult, ALU.subtract)
                i.then_inc(s_xj, 1)

            def hidden_lo(c):
                e.wait_ge(w.s.thi, w.at("t", 1))
                v.tensor_tensor(mlo[:, 2 * c:2 * c + 2, :], TB[w.n["t"] % 2][:, 0:S].rearrange("p (a s) -> p a s", s=P),
                                mhi[:, 2 * c:2 * c + 2, :].bitcast(F32), ALU.subtract).then_inc(w.s.tfree, 1)
                w.n["t"] += 1

            def add_scattered(c, job):
                e.wait_ge(s_scat, job * 2 + (c + 1))
                for t in range(T):
                    x = h[:, t, c * 512:(c + 1) * 512]
                    i = v.scalar_tensor_tensor(x, SC[t][:, :], jobcur[:, 1, t:t + 1], x, ALU.mult, ALU.add)
                i.then_inc(s_h, 1)

            last = 1 << 30
            select(jobpos[:, :, 0])
            gathered_lo(1)
            w.ring = (deep, s_deep, PANELS_A)
            split_to(w, w.n["p"] + LOOK)
            with e.Fori(0, jobs) as j:
                w.loop(j, PER_JOB)
                for c in range(FFE // 256):
                    banks = chunk(w, 4, last)
                    e.wait_ge(s_silu, j * 14 + (FF1 // 256 + c + 1))
                    x = sg[:, c % 2, 0:256]
                    v.tensor_tensor(hn[:, c % 2, 0:256], x, banks[0][:, 256:512], ALU.mult).then_inc(s_act, 1)
                    e.wait_ge(s_act, j * 14 + (FF1 // 256 + c + 1))
                    e.sem_inc(w.s.free)
                    if c >= 1:
                        hidden_lo(c - 1)
                    if c in (1, 2):
                        add_scattered(c - 1, j)
                    if c == 3:
                        e.wait_ge(s_h, j * 2 + 8)
                        w.link(v.tensor_copy(jobcur[:, 1, :], jobgate[:, :, bass.ds(j, 1)].rearrange("p t a -> p (t a)")))
                        for t in range(T):
                            e.wait_ge(w.s.thi, w.at("t", 1))
                            v.tensor_copy(selT[:, t, HD:P], TB[w.n["t"] % 2][:, HD:P]).then_inc(w.s.tfree, 1)
                            w.n["t"] += 1
                        select(jobpos[:, :, bass.ds(j + 1, 1)].rearrange("p t a -> p (t a)"))
                split_to(w, w.n["p"] + 6)
                hidden_lo(FFE // 256 - 1)
                for c in range(2):
                    if c == 1:
                        gathered_lo(j + 2)
                    banks = chunk(w, KE // 2, last)
                    e.wait_ge(s_oh, j * 2 + (c + 1))
                    v.tensor_tensor(outlo[:, c, :], banks[0][:, :], outhi[:, c, :].bitcast(F32), ALU.subtract
                                    ).then_inc(s_ol, 1)
                    e.wait_ge(s_ol, j * 2 + (c + 3))
                    e.sem_inc(w.s.free)
                w.end(("p", "g", "t", "vd"))
            w.after(jobs)
            for c in range(2):
                add_scattered(c, jobs)

            e.drain().then_inc(B.lo, SLOTS)
            e.drain().then_inc(B.free, 2)
            e.drain().then_inc(B.tfree, 2)
            e.drain().then_inc(B.sfree, 2)
            e.drain().then_inc(B.ofree, 2)
            e.drain().then_inc(s_res, 4)
            w = Walk(e, B, B.vd)
            with e.Fori(0, 2) as l:
                w.loop(l, PER_LAYER)
                last = PANELS_B
                v.tensor_copy(n2[:, :], small[:, bass.ds(l * 24 + SM["norms2"][0], 24)]).then_inc(s_par, 1)
                e.wait_ge(s_par, l + 1)
                split_to(w, LOOK)
                turned(w, lambda k: n2[:, k:k + 1], (chi, clo))
                scaled_rows(w, hn, h)
                banks = chunk(w, 4, last)
                for t in range(T):
                    w.link(v.tensor_copy(mkv[:, t, :], banks[t][:, :]))
                e.sem_inc(B.free)
                e.sem_inc(s_z2)
                turned(w, lambda k: n2[:, 8 + k:9 + k])
                for c in range(11):
                    if c < 5:
                        banks = chunk(w, 4, last)
                        for t in range(T):
                            i = v.tensor_copy(z[:, t, c * 512:(c + 1) * 512], banks[t][:, :])
                        w.link(i)
                        e.sem_inc(B.free)
                        if c == 0:
                            turned_heads(w, [(mkT, 2, 1.0)])
                        if c == 4:
                            for base in (0, 1152):
                                for t in range(T):
                                    x = z[:, t, base:base + 768].rearrange("p (a k) -> p a k", k=HD)[:, :, 0:16]
                                    a = scratch[:, 0:192].rearrange("p (a k) -> p a k", k=16)
                                    b = scratch[:, 192:384].rearrange("p (a k) -> p a k", k=16)
                                    cs = co("cosx", 16 * t, 16).unsqueeze(1).to_broadcast([P, 12, 16])
                                    s1 = co("sinx", 16 * t, 8).unsqueeze(1).to_broadcast([P, 12, 8])
                                    s2 = co("sinx", 16 * t + 8, 8).unsqueeze(1).to_broadcast([P, 12, 8])
                                    w.mark(v.tensor_tensor(a, x, cs, ALU.mult))
                                    w.mark(v.tensor_tensor(b[:, :, 0:8], x[:, :, 8:16], s1, ALU.mult))
                                    w.link(v.tensor_tensor(b[:, :, 8:16], x[:, :, 0:8], s2, ALU.mult))
                                    w.link(v.tensor_tensor(x, a, b, ALU.add))
                            e.sem_inc(B.zrdy)
                    else:
                        w.n["p"] += 4
                        split_to(w, min(w.n["p"] + LOOK, last))
                        w.n["g"] += 1
                turned_heads(w, [(qkT[:, a[0]:a[-1] + 1, :], len(a), 0.125 if kind == "q" else 1.0)
                                 for a, kind in GROUPS2])
                attention(w, [([mask["win"], mask["dil4"], mask["dil16"]], None, 0 if i % 2 else None, None)
                              for i in range(2)]
                          + [([mask["causal"]], None, 1 + i // 2 if i % 2 else None, None) for i in range(6)]
                          + [([None], None, 4 + i // 2 if i % 2 else None, None) for i in range(4)])
                for n in range(2):
                    for br in range(3):
                        banks = chunk(w, [1, 2, 1][br], last)
                        for t in range(T):
                            gt_ = gates[:, t, br * D + n * 512:br * D + (n + 1) * 512]
                            y = hn[:, t, n * 512:(n + 1) * 512]
                            if br == 0:
                                i = v.tensor_tensor(y, gt_, banks[t][:, :], ALU.mult)
                            else:
                                w.link(v.tensor_tensor(gt_, gt_, banks[t][:, :], ALU.mult))
                                i = v.tensor_tensor(y, y, gt_, ALU.add)
                        w.link(i)
                        e.sem_inc(B.free)
                e.sem_inc(s_y2)
                turned(w, None)
                for c in range(2):
                    add_rows(w, chunk(w, 4, last), c, s_res)
                norm_rows(w, h, lambda k: n2[:, 16 + k:17 + k])
                for c in range(8):
                    banks = chunk(w, 4, last)
                    for b in range(2):
                        n = 2 * c + b
                        e.wait_ge(s_r2, l * 16 + n + 1)
                        if b == 1:
                            e.sem_inc(B.free)
                        x = sg[:, b, :]
                        v.tensor_tensor(x, x, x, ALU.mult).then_inc(s_q2, 1)
                    for b in range(2):
                        n = 2 * c + b
                        e.wait_ge(s_h2, l * 16 + n + 1)
                        k = 4 * c + 2 * b
                        v.tensor_tensor(flo[:, k:k + 2, :], sg[:, b, :].rearrange("p (a s) -> p a s", s=S),
                                        fhi[:, k:k + 2, :].bitcast(F32), ALU.subtract).then_inc(s_l2, 1)
                for c in range(2):
                    add_rows(w, chunk(w, 16, last), c, s_res)
                w.end(("p", "g", "t", "n", "s", "a", "r", "o", "vd"))
            w.it = None
            w.n["n"] = 4
            e.wait_ge(B.nss, 5)
            v.tensor_scalar(stat[:, 0:T], stat[:, 0:T], 1.0 / D, EPS, ALU.mult, ALU.add).then_inc(B.nms, 1)
            e.wait_ge(B.nr, 5)
            e.wait_ge(s_gf, 16)
            for t in range(T):
                i = v.scalar_tensor_tensor(hn[:, t, :], h[:, t, :], stat[:, t:t + 1], mbuf[:, 0, :], ALU.mult, ALU.mult)
            i.then_inc(B.nhn, 1)

        @block.tensor
        def _(e):
            mm, tr = nc.tensor.matmul, nc.tensor.transpose

            def chunk_tokens(w, lhi, llo, panels, ntok=T, width=512, k0=0, before=None):
                e.wait_ge(w.s.free, w.at("g", 1))
                g, k, n = w.n["g"], k0, sum(panels)
                for step, tiles in enumerate(panels):
                    if before is not None:
                        before(step)
                    e.wait_ge(w.s.lo, w.at("p", 1 + SLOTS))
                    slot = w.n["p"] % SLOTS
                    for kk in range(tiles):
                        cols = slice(kk * 512, kk * 512 + width)
                        for t in range(ntok):
                            row = slice(t * P, (t + 1) * P)
                            for q, (x, y) in enumerate(((lhi, whi), (lhi, wlo), (llo, whi))):
                                i = mm(L[2 * (g % 2) + t][:, 0:width], x[:, k, row], y[:, slot, cols],
                                       start=(k == k0 and q == 0), stop=(k == k0 + n - 1 and q == 2))
                        k += 1
                    i.then_inc(w.s.used, 1)
                    w.n["p"] += 1
                w.n["g"] += 1

            def chunk_features(w, before=None):
                e.wait_ge(w.s.free, w.at("g", 1))
                g = w.n["g"]
                for j in range(4):
                    if before is not None:
                        before(j)
                    e.wait_ge(w.s.lo, w.at("p", 1 + SLOTS))
                    slot = w.n["p"] % SLOTS
                    for kk in range(2):
                        k = 2 * j + kk
                        for f in range(4):
                            cols = slice(kk * 512 + f * P, kk * 512 + (f + 1) * P)
                            out = L[2 * (g % 2) + f // 2][:, (f % 2) * S:(f % 2 + 1) * S]
                            for q, (x, y) in enumerate(((whi, xhi), (wlo, xhi), (whi, xlo))):
                                i = mm(out, x[:, slot, cols], y[:, k, :], start=(k == 0 and q == 0 and f % 2 == 0),
                                       stop=(k == KD - 1 and q == 2 and f % 2 == 1), skip_group_check=True)
                    i.then_inc(w.s.used, 1)
                    w.n["p"] += 1
                w.n["g"] += 1

            def turn(w, tiles):
                e.wait_ge(w.s.tfree, w.at("t", 1))
                for c, src in tiles:
                    i = tr(TB[w.n["t"] % 2][:, c:c + P], src, ident)
                i.then_inc(w.s.tdone, 1)
                w.n["t"] += 1

            def turn_rows(w, src, ready):
                def group(q):
                    turn(w, [(kk * S + t * P, src[:, t, (2 * q + kk) * P:(2 * q + kk + 1) * P])
                             for kk in range(2) for t in range(T)])

                e.wait_ge(*ready)
                for q in range(3):
                    group(q)

                def before(panel):
                    if panel == 1:
                        group(3)
                    e.wait_ge(w.s.tfree, w.at("t", max(panel - 1, 0)))
                return before

            def norm(w):
                w.n["n"] += 1
                return turn_rows(w, hn, (w.s.nhn, w.at("n")))

            def attention(w, heads):
                def scores(i):
                    for qp, row, key, _ in heads[i][0]:
                        e.wait_ge(w.s.sfree, w.at("s", 1))
                        for t in range(T):
                            ins = mm(SC[w.n["s"] % 2][:, t * S:(t + 1) * S], qkT[row:row + HD, qp, t * P:(t + 1) * P],
                                     key, start=True, stop=True)
                        ins.then_inc(w.s.sdone, 1)
                        w.n["s"] += 1

                plan = score_slots([len(x[0]) for x in heads])

                def transposes(i, j):
                    r = w.n["r"]
                    e.wait_ge(w.s.rcopy, w.at("r", 1))
                    for kt in range(2):
                        for t in range(T):
                            ins = tr(TB[r % 2][:, kt * S + t * P:kt * S + (t + 1) * P],
                                     SMX[:, plan[i][0] + j, t, kt * P:(kt + 1) * P], ident)
                    ins.then_inc(w.s.rdone, 1)
                    w.n["r"] += 1

                def values(i, j, later):
                    tiles, ends = heads[i]
                    if i % 2 == 0 and j == 0:
                        e.wait_ge(w.s.ofree, w.at("o", 1))
                    e.wait_ge(w.s.rcopy, w.at("r", 2 - later))
                    half, r = (i % 2) * HD, w.n["r"] - 1 - later
                    for kt in range(2):
                        ins = mm(output_bank(w)[half:half + HD, 0:S], tiles[j][3](kt), PT[:, r % 2, kt * S:(kt + 1) * S],
                                 start=(j == 0 and kt == 0), stop=(j == len(tiles) - 1 and kt == 1))
                    ins.then_inc(w.s.pv, 1)
                    if ends and j == len(tiles) - 1:
                        w.n["o"] += 1

                e.wait_ge(w.s.tfree, w.at("t", 2))
                scores(0)
                scores(1)
                before = None
                for i in range(len(heads)):
                    if i + 2 < len(heads):
                        scores(i + 2)
                    e.wait_ge(w.s.pr, w.at("a", i + 1))
                    for j in range(len(heads[i][0])):
                        transposes(i, j)
                        if before is not None:
                            values(*before, 1)
                        before = (i, j)
                values(*before, 0)
                w.n["a"] += len(heads)
                pairs = sum(ends for _, ends in heads)
                return lambda i: e.wait_ge(w.s.ofree, w.at("o", i + 3 - pairs))

            def mem_value(hh):
                return lambda kt: mkv[:, kt, 256 + hh * HD:256 + (hh + 1) * HD]

            def mem_heads(pair0):
                return [([(pair0 + hh // 2, (hh % 2) * HD, mkT[(hh % 2) * HD:(hh % 2 + 1) * HD, hh // 2, :],
                           mem_value(hh))], hh % 2 == 1) for hh in range(4)]

            e.drain().then_inc(A.used, SLOTS)
            e.drain().then_inc(A.rcopy, 2)
            e.drain().then_inc(A.pv, 2)
            w = Walk(e, A)
            e.wait_ge(s_in[0], 16)
            chunk_tokens(w, xhi, xlo, FULL, before=norm(w))
            e.wait_ge(A.zrdy, 1)
            turn(w, [(c * S + t * P, mkv[:, t, c * P:(c + 1) * P]) for c in range(2) for t in range(T)])
            rows = norm(w)
            def taps(c):
                e.wait_ge(s_ev, c + 2)
                e.wait_ge(s_diag, c + 1)
                if c >= 2:
                    e.wait_ge(s_conv, c - 1)
                for f in range(2):
                    for i in range(TAPS_PE):
                        tap = TAPS_V + i
                        ins = mm(SC[c % 2][:, f * S:(f + 1) * S], diag[2 * c + f][:, i, :], u[:, 2 * c + f, tap:tap + S],
                                 start=(i == 0), stop=(i == TAPS_PE - 1))
                ins.then_inc(s_tap, 1)

            chunk_features(w, before=rows)
            for c in range(2):
                chunk_features(w)
                taps(c)
            chunk_tokens(w, xhi, xlo, FULL, width=256)
            taps(2)
            e.wait_ge(A.zrdy, 2)
            turn(w, [(c * S + t * P, z[:, t, c * P:(c + 1) * P]) for c in range(2) for t in range(T)])
            for q in range(3):
                e.wait_ge(s_conv, q + 1)
                turn(w, [(t * S + kk * P, cacc[:, 2 * q + kk, t * P:(t + 1) * P]) for kk in range(2) for t in range(T)])
            e.wait_ge(s_ln, 5)
            for q in range(3):
                turn(w, [(kk * S + t * P, ctok[:, t, (2 * q + kk) * P:(2 * q + kk + 1) * P])
                         for kk in range(2) for t in range(T)])
            placed = attention(w, mem_heads(0))
            for c in range(2):
                chunk_tokens(w, chi, clo, FULL, before=lambda i: placed(1) if i == 3 else None)
            rows = norm(w)
            for c in range(FF1 // 256):
                chunk_features(w, before=rows if c == 0 else None)
            w.n["n"] += 1
            for c in range(2):
                chunk_tokens(w, fhi, flo, [2] * (FF1 // 256),
                             before=lambda i: e.wait_ge(s_frdy, i + 1))
            rows = norm(w)
            for c in range(3):
                chunk_tokens(w, xhi, xlo, FULL, before=rows if c == 0 else None)
            e.wait_ge(A.zrdy, 5)

            for i in range(3):
                turn(w, [(c * S + t * P, z[:, t, (2 * i + c) * P:(2 * i + c + 1) * P]) for c in range(2) for t in range(T)])
            for base in (768, 1280):
                turn(w, [(c * S + t * P, z[:, t, base + c * P:base + (c + 1) * P]) for c in range(2) for t in range(T)])

            def window_head(i):
                kv = i // 3
                row = (kv % 2) * HD
                return ([((kv // 2) * 3 + i % 3, row, qkT[row:row + HD, 6 + kv // 2, :],
                          lambda kt: z[:, kt, 1024 + kv * HD:1024 + (kv + 1) * HD])], i % 2 == 1)
            placed = attention(w, [window_head(i) for i in range(12)] + mem_heads(8))
            for c in range(2):
                chunk_tokens(w, chi, clo, FULL, before=lambda i: placed(2 * i + 1))
            rows = norm(w)
            for q in range(4):
                rows(q)
            e.wait_ge(s_pre, 6)
            for t in range(T):
                for k in range(KD):
                    for q, (x, y) in enumerate(((xhi, rhi), (xhi, rlo), (xlo, rhi))):
                        i = mm(SC[0][:, t * NE:(t + 1) * NE], x[:, k, t * P:(t + 1) * P], y[:, k * NE:(k + 1) * NE],
                               start=(k == 0 and q == 0), stop=(k == KD - 1 and q == 2))
            i.then_inc(s_rt, 1)
            e.wait_ge(s_rv, 1)
            tri = co("tri")
            pick = [scratch[:, 40 + 8 * t:48 + 8 * t] for t in range(T)]
            mm(SC[1][:, 0:8], tri, pick[0], start=True, stop=True)
            mm(SC[1][:, 8:16], co("ones"), pick[0], start=True, stop=False)
            mm(SC[1][:, 8:16], tri, pick[1], start=False, stop=True)
            mm(SC[1][:, 16:24], co("ones"), pick[0], start=True, stop=False)
            mm(SC[1][:, 16:24], co("ones"), pick[1], start=False, stop=True).then_inc(s_rt, 1)
            e.wait_ge(s_tab, 1)
            jobs = e.value_load(tab[0:1, 0:1], min_val=1, max_val=MAXJOB - 1)

            def gather(n):
                e.wait_ge(s_sel, n)
                for k in range(KD):
                    out = SC[k // 4][:, (k % 4) * P:(k % 4 + 1) * P]
                    for t in range(T):
                        for q, x in enumerate((tokhi, toklo)):
                            i = mm(out, x[:, t, k * P:(k + 1) * P], sel[:, t, :], start=(t == 0 and q == 0),
                                   stop=(t == 1 and q == 1))
                i.then_inc(s_gat, 1)

            def scatter(c):
                for t in range(T):
                    for q, y in enumerate((outhi, outlo)):
                        i = mm(SC[t][:, :], selT[:, t, :], y[:, c, :], start=(q == 0), stop=(q == 1))
                i.then_inc(s_scat, 1)

            e.wait_ge(s_tokl, 1)
            gather(1)
            with e.Fori(0, jobs) as j:
                w.loop(j, PER_JOB)
                e.wait_ge(s_xj, j + 1)

                def turn_hidden(c):
                    e.wait_ge(s_act, j * 14 + (FF1 // 256 + c + 1))
                    turn(w, [(kk * P, hn[:, c % 2, kk * P:(kk + 1) * P]) for kk in range(2)])

                for c in range(FFE // 256):
                    chunk_tokens(w, xhi, xlo, FULL, ntok=1)
                    if c >= 1:
                        turn_hidden(c - 1)
                    if c == 1:
                        e.wait_ge(s_ol, j * 2 + 2)
                        scatter(0)
                    if c == 2:
                        e.wait_ge(s_h, j * 2 + 7)
                        scatter(1)
                    if c == 3:
                        for t in range(T):
                            turn(w, [(0, sel[:, t, :].bitcast(F32))])

                def hidden_ready(i):
                    if i == 0:
                        e.wait_ge(w.s.tfree, w.at("t", 1))
                    if i == 3:
                        turn_hidden(FFE // 256 - 1)
                    if i == 12:
                        e.wait_ge(w.s.tfree, w.at("t", 1))
                    if i == 13:
                        e.wait_ge(w.s.tfree, w.at("t", 2))

                chunk_tokens(w, mhi, mlo, [2] * (KE // 2), ntok=1, before=hidden_ready)
                e.wait_ge(s_h, j * 2 + 8)
                gather(j + 2)
                chunk_tokens(w, mhi, mlo, [2] * (KE // 2), ntok=1)
                w.end("pgt")
            e.wait_ge(s_ol, jobs * 2 + 2)
            e.wait_ge(s_xj, jobs + 1)
            scatter(0)
            e.wait_ge(s_h, jobs * 2 + 7)
            scatter(1)

            e.wait_ge(s_res, 4)
            e.drain().then_inc(B.used, SLOTS)
            e.drain().then_inc(B.rcopy, 2)
            e.drain().then_inc(B.pv, 2)
            w = Walk(e, B)
            with e.Fori(0, 2) as l:
                w.loop(l, PER_LAYER)
                e.wait_ge(s_par, l + 1)
                chunk_tokens(w, chi, clo, FULL, before=turn_rows(w, mbuf, (A.nhn, 4)))
                rows = norm(w)
                for c in range(11):
                    chunk_tokens(w, xhi, xlo, FULL, before=rows if c == 0 else None)
                    if c == 0:
                        e.wait_ge(s_z2, l + 1)
                        turn(w, [(c * S + t * P, mkv[:, t, c * P:(c + 1) * P]) for c in range(2) for t in range(T)])
                e.wait_ge(B.zrdy, l + 1)
                for pairs, _ in GROUPS2:
                    turn(w, [(c * S + t * P, z[:, t, PAIRS2[a]:PAIRS2[a] + P]) for c, a in enumerate(pairs)
                             for t in range(T)])
                e.wait_ge(B.tfree, w.at("t", 2))

                def head2(x, q0, k0, vcol):
                    row = (x % 2) * HD
                    return (q0 + x // 2, row, qkT[row:row + HD, k0 + x // 2, :],
                            lambda kt: z[:, kt, vcol + x * HD:vcol + (x + 1) * HD])
                placed = attention(w, [([head2(2 * g + i, 0, 3, 768) for g in range(3)], i == 1) for i in range(2)]
                          + [([head2(x, 6, 9, 1920)], x % 2 == 1) for x in range(6)] + mem_heads(12))
                for n in range(2):
                    placed(0)
                    chunk_tokens(w, chi, clo, [1], k0=0)
                    placed(5)
                    chunk_tokens(w, chi, clo, [2, 1], k0=1)
                    chunk_tokens(w, chi, clo, [2], k0=4)
                rows = turn_rows(w, hn, (s_y2, l + 1))
                for c in range(2):
                    chunk_tokens(w, xhi, xlo, FULL, before=rows if c == 0 else None)
                rows = norm(w)
                for c in range(8):
                    chunk_features(w, before=rows if c == 0 else None)
                for c in range(2):
                    chunk_tokens(w, fhi, flo, [2] * 16,
                                 before=lambda i: e.wait_ge(s_l2, l * 16 + (i + 1)))
                w.end("pgtnsaro")


def chunks_of(w, width=512):
    k, n = w.shape
    kp, nc_ = -(-k // 256), -(-n // 512)
    out = np.zeros((nc_, kp, P, 2, 512), w.dtype)
    for c in range(nc_):
        cols = w[:, c * 512:(c + 1) * 512]
        for i in range(k // P):
            out[c, i // 2, :, i % 2, 0:cols.shape[1]] = cols[i * P:(i + 1) * P]
    return out.reshape(nc_ * kp, P, 1024)


def paired(a, b):
    k, n = a.shape
    both = np.stack([x.reshape(k // 256, 2, P, n // 256, 256).transpose(3, 0, 2, 1, 4) for x in (a, b)], axis=4)
    return both.reshape(n // 256 * (k // 256), P, 1024)


def tiles(v):
    return v.reshape(-1, P).T


def constants():
    i = np.arange(P)
    tok = np.arange(S)
    dist = (tok[:, None] - tok[None, :]).astype(np.float32)
    rows = lambda m: m.reshape(T, P, S).transpose(1, 0, 2).reshape(P, T * S)
    blocked = lambda ok: rows(np.where(ok, np.float32(0), np.float32(-1e30)))
    causal = dist >= 0
    e8 = np.arange(NE)
    inv = (1.0 / (np.float32(500000.0) ** (np.arange(0, 16, 2, dtype=np.float32) / np.float32(16)))).astype(np.float32)
    ang = tok.astype(np.float32)[:, None] * inv[None, :]
    cos, sin = np.cos(ang).astype(np.float32), np.sin(ang).astype(np.float32)
    per = lambda m: m.reshape(T, P, 16).transpose(1, 0, 2).reshape(P, T * 16)
    wide = lambda v: np.broadcast_to(v.reshape(1, -1), (P, v.size))
    c = dict(
        ident=np.eye(P), tri=(i[:, None] < i[None, :]), ones=np.ones((P, P)), iota=wide(i),
        slope=wide(-np.exp2(-8.0 * (np.arange(12) + 1.0) / 12)),
        low=wide((e8[None, :] < e8[:, None]).astype(np.float32)),
        jobs=wide(np.repeat(np.arange(MAXJOB), NE)), experts=wide(np.tile(e8, MAXJOB)),
        dist=rows(np.where(causal & (dist < 128), dist, np.float32(1e33))),
        win=blocked(causal & (dist <= 128)), dil4=blocked(causal & (dist % 4 == 0)),
        dil16=blocked(causal & (dist % 16 == 0)), causal=blocked(causal),
        cosx=per(np.concatenate([cos, cos], 1)), sinx=per(np.concatenate([-sin, sin], 1)))
    return np.ascontiguousarray(np.concatenate([np.asarray(c[k], np.float32).reshape(P, n) for k, n in CONST.items()], 1))


def kernel(**a):
    import concourse.bacc as bacc
    from concourse.bass_utils import run_bass_kernel_spmd as run
    a = {k: np.asarray(v) for k, v in a.items()}
    two = lambda g: np.concatenate([g, g]).reshape(P, 1)
    cv, sw = a["cv_w_in"][0], a["sw_w_in"][0]
    order = [x + 3 * y + 6 * g for g in range(2) for x in range(3) for y in range(2)]
    sw = np.concatenate([sw[:, i * HD:(i + 1) * HD] for i in order] + [sw[:, 768:]], 1)
    w1 = np.concatenate([
        chunks_of(a["w_mem_kv"]), paired(cv[:, 0:CONV], cv[:, CONV:2 * CONV]), chunks_of(cv[:, 2 * CONV:]),
        chunks_of(a["cv_w_out"][0]), paired(a["cv_w_gate"][0], a["cv_w_up"][0]), chunks_of(a["cv_w_down"][0]),
        chunks_of(sw), chunks_of(a["sw_w_out"][0])])
    wm = np.concatenate([x for e in range(NE) for x in (
        paired(a["sw_we_gate"][0, e], a["sw_we_up"][0, e]), chunks_of(a["sw_we_down"][0, e]))])
    w2 = []
    for l in range(2):
        pa, pb, pm = (chunks_of(a[f"w_proj_{b}_2"][l]) for b in "abm")
        w2 += [chunks_of(a["w_mem_kv_2"][l]), chunks_of(a["w_in_2"][l])]
        for n in range(2):
            w2 += [pa[n:n + 1], pb[2 * n:2 * n + 2], pm[n:n + 1]]
        w2 += [chunks_of(a["w_out_2"][l]), chunks_of(a["w_up_2"][l]), chunks_of(a["w_down_2"][l])]
    w2 = np.concatenate(w2)
    parts = dict(
        mem_g=tiles(a["mem_norm_g"]), cvn=tiles(a["cv_attn_norm_g"][0]), cvf=tiles(a["cv_ffn_norm_g"][0]),
        swn=tiles(a["sw_attn_norm_g"][0]), swf=tiles(a["sw_ffn_norm_g"][0]), bglu=tiles(a["cv_b_glu"][0]),
        dww=a["cv_dw_w"][0].reshape(TAPS, FC, P).transpose(2, 1, 0).reshape(P, FC * TAPS),
        dwb=tiles(a["cv_dw_b"][0]), lng=tiles(a["cv_ln_g"][0]), lnb=tiles(a["cv_ln_b"][0]),
        memk=two(a["mem_k_norm_g"]), cvq=two(a["cv_memq_norm_g"][0]), swmq=two(a["sw_memq_norm_g"][0]),
        swq=two(a["sw_q_norm_g"][0]), swk=two(a["sw_k_norm_g"][0]),
        sinks=np.broadcast_to(a["sw_sinks"][0].reshape(1, 12), (P, 12)),
        router=a["sw_router"][0].reshape(KD, P, NE).transpose(1, 0, 2).reshape(P, KD * NE),
        norms2=np.concatenate([tiles(a[k][l]) for l in range(2) for k in ("norm_mem_2", "norm_mix_2", "norm_mlp_2")], 1))
    small = np.concatenate([parts[k] for k in SMALL], 1)
    arrays = dict(x=a["x"][0], mem=a["mem"][0], mem2=a["mem_2"][0], w1=w1, wm=wm, w2=w2, small=small,
                  const=constants(), gfin=np.broadcast_to(a["norm_final_2"].reshape(1, D), (P, D)))
    arrays = {k: np.ascontiguousarray(v) for k, v in arrays.items()}
    nc = bacc.Bacc("TRN2", target_bir_lowering=False, num_devices=1)
    d = {k: nc.dram_tensor(k, v.shape, mybir.dt.from_np(v.dtype), kind="ExternalInput").ap() for k, v in arrays.items()}
    d["out"] = nc.dram_tensor("out", (S, D), F32, kind="ExternalOutput").ap()
    build(nc, d)
    r = run(nc, [arrays], core_ids=[0])
    return r.results[0]["out"].reshape(1, S, D)
```
